# Optimizing a Trainium2 kernel written in Bass

```python
import math
import jax
import jax.numpy as jnp
from jax import lax
import numpy as np

D_MODEL = 1024
BATCH = 1
SEQ = 128
DEPTH = 1
DEC_BATCH = 1
DEC_SEQ = 512
PAST_LEN = 128

GRID_W = 64
HEAD_DIM = 64
NA_HEADS = D_MODEL // (2 * HEAD_DIM)
DIFF_HEADS = D_MODEL // (4 * HEAD_DIM)
NA_WIDTH = NA_HEADS * HEAD_DIM
DIFF_WIDTH = DIFF_HEADS * 2 * HEAD_DIM
MIX_WIDTH = NA_WIDTH + DIFF_WIDTH
QKV_WIDTH = 3 * NA_WIDTH + 3 * DIFF_WIDTH
NA_WIN_H = 8
NA_WIN_W = 16
N_EXPERTS = 16
EC_CAPACITY_FACTOR = 2
D_FF = int(math.ceil(8 * D_MODEL / 3 / 128)) * 128
ROPE_THETA = 10000.0
Q_BLOCK = 128
NORM_EPS = 1e-5
NEG_INF = -1e30
DEEPNORM_ALPHA = (2.0 * DEPTH) ** 0.25
DEEPNORM_BETA = (8.0 * DEPTH) ** -0.25

kernel_name = "hybrid_na_diffattn_ec_moe_dit_step"

def _layer_norm(x, g, b):
    xf = x.astype(jnp.float32)
    mu = jnp.mean(xf, axis=-1, keepdims=True)
    var = jnp.mean(jnp.square(xf - mu), axis=-1, keepdims=True)
    return ((xf - mu) * lax.rsqrt(var + NORM_EPS)).astype(x.dtype) * g + b

def _rms_norm(x, g):
    xf = x.astype(jnp.float32)
    return (xf * lax.rsqrt(jnp.mean(xf * xf, axis=-1, keepdims=True) + NORM_EPS)).astype(x.dtype) * g

def _modulation(cvec, w_ada, b_ada):
    m = jax.nn.silu(cvec) @ w_ada + b_ada
    return jnp.split(m[..., None, :], 6, axis=-1)

def _axial_rope(n_tokens):
    t = jnp.arange(n_tokens)
    row = (t // GRID_W).astype(jnp.float32)
    col = (t % GRID_W).astype(jnp.float32)
    half = HEAD_DIM // 2
    inv = ROPE_THETA ** (-jnp.arange(0, half, 2, dtype=jnp.float32) / half)
    ang_r = row[:, None] * inv[None, :]
    ang_c = col[:, None] * inv[None, :]
    ang = jnp.concatenate([ang_r, ang_r, ang_c, ang_c], axis=-1)
    return jnp.cos(ang), jnp.sin(ang)

def _rot_half(x):
    x1, x2 = jnp.split(x, 2, axis=-1)
    return jnp.concatenate([-x2, x1], axis=-1)

def _apply_rope(x, cos, sin):
    xr, xc = jnp.split(x, 2, axis=-1)
    rot = jnp.concatenate([_rot_half(xr), _rot_half(xc)], axis=-1)
    return x * cos.astype(x.dtype) + rot * sin.astype(x.dtype)

def _project(h, w_in):
    b, s, _ = h.shape
    qkv = h @ w_in
    cuts = [NA_WIDTH, 2 * NA_WIDTH, 3 * NA_WIDTH,
            3 * NA_WIDTH + DIFF_WIDTH, 3 * NA_WIDTH + 2 * DIFF_WIDTH]
    na_q, na_k, na_v, df_q, df_k, df_v = jnp.split(qkv, cuts, axis=-1)

    def na_heads(t):
        return t.reshape(b, s, NA_HEADS, HEAD_DIM).transpose(0, 2, 1, 3)

    def diff_qk(t):
        return t.reshape(b, s, DIFF_HEADS, 2, HEAD_DIM).transpose(0, 2, 3, 1, 4)

    df_v = df_v.reshape(b, s, DIFF_HEADS, 2 * HEAD_DIM).transpose(0, 2, 1, 3)
    return na_heads(na_q), na_heads(na_k), na_heads(na_v), diff_qk(df_q), diff_qk(df_k), df_v

def _dense_attention(q, k, v):
    b, h, sq, d = q.shape
    nblk = sq // Q_BLOCK
    qb = q.reshape(b, h, nblk, Q_BLOCK, d).transpose(2, 0, 1, 3, 4)

    def block(qblk):
        s = jnp.einsum("bhqd,bhkd->bhqk", qblk, k, preferred_element_type=jnp.float32) * (d ** -0.5)
        p = jax.nn.softmax(s, axis=-1).astype(v.dtype)
        return jnp.einsum("bhqk,bhkd->bhqd", p, v)

    o = lax.map(block, qb)
    return o.transpose(1, 2, 0, 3, 4).reshape(b, h, sq, d)

def _diff_attention(q, k, v, lam):
    b, h, _, sq, d = q.shape
    nblk = sq // Q_BLOCK
    qb = q.reshape(b, h, 2, nblk, Q_BLOCK, d).transpose(3, 0, 1, 2, 4, 5)

    def block(qblk):
        s = jnp.einsum("bhmqd,bhmkd->bhmqk", qblk, k, preferred_element_type=jnp.float32) * (d ** -0.5)
        p = jax.nn.softmax(s, axis=-1)
        a = (p[:, :, 0] - lam * p[:, :, 1]).astype(v.dtype)
        return jnp.einsum("bhqk,bhke->bhqe", a, v)

    o = lax.map(block, qb)
    return o.transpose(1, 2, 0, 3, 4).reshape(b, h, sq, 2 * d)

def _neighbourhood_attention(q, k, v, k_ctx, v_ctx, rpb):
    b, h, s, d = q.shape
    rows = s // GRID_W
    kh = min(NA_WIN_H, rows)
    kw = NA_WIN_W
    r = jnp.arange(rows)
    w = jnp.arange(GRID_W)
    r0 = jnp.clip(r - kh // 2, 0, rows - kh)
    band_rows = r0[:, None] + jnp.arange(kh)[None, :]
    c0 = jnp.clip(w - kw // 2, 0, GRID_W - kw)
    in_win = (w[None, :] >= c0[:, None]) & (w[None, :] < c0[:, None] + kw)
    row_off = band_rows - r[:, None] + (NA_WIN_H - 1)
    col_off = jnp.clip(w[None, :] - w[:, None], -(kw - 1), kw - 1) + (NA_WIN_W - 1)
    bias = rpb[:, row_off[:, None, :, None], col_off[None, :, None, :]]

    qg = q.reshape(b, h, rows, GRID_W, d)
    kg = k.reshape(b, h, rows, GRID_W, d)[:, :, band_rows]
    vg = v.reshape(b, h, rows, GRID_W, d)[:, :, band_rows]
    scale = d ** -0.5
    s_loc = jnp.einsum("bhrwd,bhrijd->bhrwij", qg, kg, preferred_element_type=jnp.float32) * scale
    s_loc = s_loc + bias[None].astype(jnp.float32)
    s_loc = jnp.where(in_win[None, None, None, :, None, :], s_loc, NEG_INF)
    s_ctx = jnp.einsum("bhrwd,bhld->bhrwl", qg, k_ctx, preferred_element_type=jnp.float32) * scale
    n_loc = kh * GRID_W
    s_all = jnp.concatenate([s_loc.reshape(b, h, rows, GRID_W, n_loc), s_ctx], axis=-1)
    p = jax.nn.softmax(s_all, axis=-1).astype(v.dtype)
    p_loc = p[..., :n_loc].reshape(b, h, rows, GRID_W, kh, GRID_W)
    p_ctx = p[..., n_loc:]
    o = (jnp.einsum("bhrwij,bhrijd->bhrwd", p_loc, vg)
         + jnp.einsum("bhrwl,bhld->bhrwd", p_ctx, v_ctx))
    return o.reshape(b, h, s, d)

def _merge_heads(na_o, df_o, subln_g, lambda_init, w_out):
    b, _, s, _ = na_o.shape
    df_o = _rms_norm(df_o, subln_g) * (1.0 - lambda_init)
    o = jnp.concatenate([na_o.transpose(0, 2, 1, 3).reshape(b, s, NA_WIDTH),
                         df_o.transpose(0, 2, 1, 3).reshape(b, s, DIFF_WIDTH)], axis=-1)
    return o @ w_out

def _context_attention(h, w_in, w_out, lam, lambda_init, subln_g):
    na_q, na_k, na_v, df_q, df_k, df_v = _project(h, w_in)
    na_o = _dense_attention(na_q, na_k, na_v)
    df_o = _diff_attention(df_q, df_k, df_v, lam)
    out = _merge_heads(na_o, df_o, subln_g, lambda_init, w_out)
    return out, na_k, na_v, df_k, df_v

def _latent_attention(h, ck_na, cv_na, ck_df, cv_df, w_in, w_out, rpb, lam, lambda_init, subln_g):
    s = h.shape[1]
    na_q, na_k, na_v, df_q, df_k, df_v = _project(h, w_in)
    cos, sin = _axial_rope(s)
    df_q = _apply_rope(df_q, cos, sin)
    df_k = _apply_rope(df_k, cos, sin)
    na_o = _neighbourhood_attention(na_q, na_k, na_v, ck_na, cv_na, rpb)
    df_o = _diff_attention(df_q,
                           jnp.concatenate([ck_df, df_k], axis=3),
                           jnp.concatenate([cv_df, df_v], axis=2), lam)
    return _merge_heads(na_o, df_o, subln_g, lambda_init, w_out)

def _expert_choice_ffn(h, w_router, w_gate, w_up, w_down):
    b, n, d = h.shape
    cap = EC_CAPACITY_FACTOR * n // N_EXPERTS
    aff = jax.nn.softmax(jnp.einsum("bnd,de->bne", h, w_router,
                                    preferred_element_type=jnp.float32), axis=-1)
    g, idx = lax.top_k(jnp.swapaxes(aff, 1, 2), cap)
    xs = jax.vmap(lambda hb, ib: hb[ib])(h, idx)
    a = jnp.einsum("becd,edf->becf", xs, w_gate)
    u = jnp.einsum("becd,edf->becf", xs, w_up)
    y = jnp.einsum("becf,efd->becd", jax.nn.silu(a) * u, w_down) * g[..., None].astype(h.dtype)
    return jax.vmap(lambda yb, ib: jnp.zeros((n, d), h.dtype).at[ib.reshape(-1)].add(yb.reshape(-1, d)))(y, idx)

def setup_inputs(seed: int = 0) -> dict:
    key = jax.random.key(seed)
    ks = jax.random.split(key, 26)
    f32 = jnp.float32
    nrm = lambda k, shape: jax.random.normal(k, shape, f32)
    nrel_h, nrel_w = 2 * NA_WIN_H - 1, 2 * NA_WIN_W - 1
    return {
        "x_prompt": nrm(ks[0], (BATCH, SEQ, D_MODEL)),
        "x_sample": nrm(ks[1], (DEC_BATCH, DEC_SEQ, D_MODEL)),
        "cache_na_k": nrm(ks[2], (DEC_BATCH, DEPTH, NA_HEADS, PAST_LEN, HEAD_DIM)),
        "cache_na_v": nrm(ks[3], (DEC_BATCH, DEPTH, NA_HEADS, PAST_LEN, HEAD_DIM)),
        "cache_diff_k": nrm(ks[4], (DEC_BATCH, DEPTH, DIFF_HEADS, 2, PAST_LEN, HEAD_DIM)),
        "cache_diff_v": nrm(ks[5], (DEC_BATCH, DEPTH, DIFF_HEADS, PAST_LEN, 2 * HEAD_DIM)),
        "c": nrm(ks[6], (DEC_BATCH, D_MODEL)),
        "c_ctx": nrm(ks[7], (D_MODEL,)),
        "w_ada": nrm(ks[8], (DEPTH, D_MODEL, 6 * D_MODEL)) * (0.5 * D_MODEL ** -0.5),
        "b_ada": nrm(ks[9], (DEPTH, 6 * D_MODEL)) * 0.01,
        "w_in": nrm(ks[10], (DEPTH, D_MODEL, QKV_WIDTH)) * D_MODEL ** -0.5,
        "w_out": nrm(ks[11], (DEPTH, MIX_WIDTH, D_MODEL)) * (MIX_WIDTH ** -0.5 * DEEPNORM_BETA),
        "na_rel_bias": nrm(ks[12], (DEPTH, NA_HEADS, nrel_h, nrel_w)) * 0.1,
        "lambda_q1": nrm(ks[13], (DEPTH, HEAD_DIM)) * 0.1,
        "lambda_k1": nrm(ks[14], (DEPTH, HEAD_DIM)) * 0.1,
        "lambda_q2": nrm(ks[15], (DEPTH, HEAD_DIM)) * 0.1,
        "lambda_k2": nrm(ks[16], (DEPTH, HEAD_DIM)) * 0.1,
        "subln_g": 1.0 + 0.01 * nrm(ks[17], (DEPTH, 2 * HEAD_DIM)),
        "ln1_g": 1.0 + 0.01 * nrm(ks[18], (DEPTH, D_MODEL)),
        "ln1_b": 0.01 * nrm(ks[19], (DEPTH, D_MODEL)),
        "ln2_g": 1.0 + 0.01 * nrm(ks[20], (DEPTH, D_MODEL)),
        "ln2_b": 0.01 * nrm(ks[21], (DEPTH, D_MODEL)),
        "w_router": nrm(ks[22], (DEPTH, D_MODEL, N_EXPERTS)) * D_MODEL ** -0.5,
        "w_gate": nrm(ks[23], (DEPTH, N_EXPERTS, D_MODEL, D_FF)) * D_MODEL ** -0.5,
        "w_up": nrm(ks[24], (DEPTH, N_EXPERTS, D_MODEL, D_FF)) * D_MODEL ** -0.5,
        "w_down": nrm(ks[25], (DEPTH, N_EXPERTS, D_FF, D_MODEL)) * (D_FF ** -0.5 * DEEPNORM_BETA),
    }

def reference(x_prompt, x_sample, cache_na_k, cache_na_v, cache_diff_k, cache_diff_v, c, c_ctx,
              w_ada, b_ada, w_in, w_out, na_rel_bias, lambda_q1, lambda_k1, lambda_q2, lambda_k2,
              subln_g, ln1_g, ln1_b, ln2_g, ln2_b, w_router, w_gate, w_up, w_down):
    xp = x_prompt
    xs = x_sample
    na_k_list, na_v_list, df_k_list, df_v_list = [], [], [], []
    for l in range(DEPTH):
        lambda_init = 0.8 - 0.6 * math.exp(-0.3 * l)
        lam = (jnp.exp(jnp.sum((lambda_q1[l] * lambda_k1[l]).astype(jnp.float32)))
               - jnp.exp(jnp.sum((lambda_q2[l] * lambda_k2[l]).astype(jnp.float32)))
               + lambda_init)

        sh1, sc1, g1, sh2, sc2, g2 = _modulation(c_ctx, w_ada[l], b_ada[l])
        a, nk, nv, dk, dv = _context_attention(xp * (1.0 + sc1) + sh1, w_in[l], w_out[l],
                                               lam, lambda_init, subln_g[l])
        xp = _layer_norm(DEEPNORM_ALPHA * xp + g1 * a, ln1_g[l], ln1_b[l])
        f = _expert_choice_ffn(xp * (1.0 + sc2) + sh2, w_router[l], w_gate[l], w_up[l], w_down[l])
        xp = _layer_norm(DEEPNORM_ALPHA * xp + g2 * f, ln2_g[l], ln2_b[l])
        na_k_list.append(nk)
        na_v_list.append(nv)
        df_k_list.append(dk)
        df_v_list.append(dv)

        sh1, sc1, g1, sh2, sc2, g2 = _modulation(c, w_ada[l], b_ada[l])
        a = _latent_attention(xs * (1.0 + sc1) + sh1, cache_na_k[:, l], cache_na_v[:, l],
                              cache_diff_k[:, l], cache_diff_v[:, l], w_in[l], w_out[l],
                              na_rel_bias[l], lam, lambda_init, subln_g[l])
        xs = _layer_norm(DEEPNORM_ALPHA * xs + g1 * a, ln1_g[l], ln1_b[l])
        f = _expert_choice_ffn(xs * (1.0 + sc2) + sh2, w_router[l], w_gate[l], w_up[l], w_down[l])
        xs = _layer_norm(DEEPNORM_ALPHA * xs + g2 * f, ln2_g[l], ln2_b[l])

    new_na_k = jnp.stack(na_k_list, axis=1)
    new_na_v = jnp.stack(na_v_list, axis=1)
    new_diff_k = jnp.stack(df_k_list, axis=1)
    new_diff_v = jnp.stack(df_v_list, axis=1)
    return (xp, xs, new_na_k, new_na_v, new_diff_k, new_diff_v)


_drawn_inputs = setup_inputs


def setup_inputs(seed=0):
    import zlib

    import numpy as np

    out = dict(_drawn_inputs(seed))
    spreads = {}
    factors = {'cache_na_k': 8.0,
     'cache_na_v': 7.101,
     'cache_diff_k': 5.381,
     'cache_diff_v': 4.487,
     'b_ada': 4.227,
     'na_rel_bias': 64.0,
     'lambda_q1': 8.0,
     'lambda_k1': 200.0,
     'lambda_q2': 8.0,
     'lambda_k2': 8.0,
     'subln_g': 192.188,
     'ln1_g': 5.6,
     'ln1_b': 17.691,
     'ln2_g': 188.074,
     'ln2_b': 187.682}
    for name, (base, spread) in spreads.items():
        noise = np.random.default_rng([zlib.crc32(name.encode()), seed]).standard_normal(out[name].shape)
        drawn = base * np.exp(spread * noise) if base else spread * noise
        out[name] = jnp.asarray(drawn.astype(out[name].dtype))
    for name, factor in factors.items():
        out[name] = (out[name] * factor).astype(out[name].dtype)
    return out
```

```python
import math
from contextlib import ExitStack

import numpy as np

import concourse.bass as bass
from concourse import mybir
from concourse.alu_op_type import AluOpType as ALU

F32 = mybir.dt.float32
ACT = mybir.ActivationFunctionType
AX_X = mybir.AxisListType.X

P = 128
D = 1024
KT = D // P
CTX = 128
LAT = 512
TOK = CTX + LAT
TT = TOK // P
GRID = 64
ROWS = LAT // GRID
HD = 64
GROUPS = 4
WIN_H, WIN_W = 8, 16
DR = 2 * WIN_H - 1
DC = 2 * WIN_W - 1
BX = DR + 1
E = 16
CAP_L = 2 * LAT // E
CAP_C = 2 * CTX // E
CAP = CAP_L + CAP_C
CAPW = 96
FF = 2816
FT = FF // P
CW = 2048
FPC = 2
NC_F = FT // FPC
RING = 11
ADA_CHUNKS = 24
OUT_CHUNKS = 4
FIRST_EXPERT_CHUNK = ADA_CHUNKS + OUT_CHUNKS
PER_PAIR = 2 * 3 * NC_F
EXPERT_CHUNKS = E * 3 * NC_F
PAIRS = E // 2
ALPHA = 2.0 ** 0.25
EPS = 1e-5
LAMBDA_INIT = 0.8 - 0.6 * math.exp(-0.3 * 0)
SCALE = HD ** -0.5
NEG = -1e30
PRIMED = 1


class Tally:

    def __init__(self, sem):
        self.sem, self.base, self.i, self.per, self.k = sem, 0, None, 0, 0

    def enter(self, i, per):
        self.base, self.i, self.per, self.k = self.base + self.k, i, per, 0

    def leave(self, iterations):
        assert self.k == self.per, (self.k, self.per)
        self.base, self.i, self.k = self.base + self.per * iterations, None, 0

    def value(self):
        return self.base + self.k if self.i is None else self.i * self.per + (self.base + self.k)


def units():
    out, s = [], 0
    for h in range(2):
        for t in range(TT):
            out.append(("na", h, t, 640 if t else CTX, [s]))
            s += 1
    for t in range(TT):
        out.append(("df", 0, t, 640 if t else CTX, [s, s + 1]))
        s += 2
    return out, s


def build(nc, a):
    ctx = ExitStack()
    with ctx:
        def sem(name):
            return ctx.enter_context(nc.semaphore(name))

        ring = ctx.enter_context(nc.sbuf_tensor("ring", [P, RING, CW], F32))
        ARENA = 30600
        arena = ctx.enter_context(nc.sbuf_tensor("arena", [P, ARENA], F32))
        ps = ctx.enter_context(nc.psum_tensor("ps", [P, 8, 512], F32))
        bias_scratch = nc.dram_tensor("bias_scratch", [GROUPS, P, 2 * BX * GRID], F32, kind="Internal").ap()
        gate_scratch = nc.dram_tensor("gate_scratch", [2, KT, P], F32, kind="Internal").ap()

        top = [0]

        def take(n):
            at = top[0]
            top[0] += n
            assert top[0] <= ARENA, top[0]
            return arena[:, at:at + n]

        ident = take(P)
        modT = take(6 * KT * 2).rearrange("p (m k v) -> p m k v", m=6, k=KT)
        wroute = take(KT * E).rearrange("p (k e) -> p k e", k=KT)
        iota1 = take(CAP_L)
        subg = take(P)
        lam_s = take(8)
        cosT = take(LAT)
        sinT = take(LAT)
        rotM = take(P)
        silu_c = take(2 * KT).rearrange("p (k v) -> p k v", k=KT)
        badaT = take(6 * KT).rearrange("p (m k) -> p m k", m=6)
        stat = take(20 * 4).rearrange("p (s c) -> p s c", c=4)
        rec = take(15 * 2).rearrange("p (s c) -> p s c", c=2)
        bnst = take(12).rearrange("p (a c) -> p a c", a=2)
        bnag = take(4)
        rms = take(3 * 20).rearrange("p (c n) -> p c n", c=3)
        xT = take(KT * TOK).rearrange("p (k t) -> p k t", k=KT)
        x1 = xT.rearrange("p k t -> p (k t)").rearrange("p (t d) -> p t d", t=TT)
        O = take(TT * D).rearrange("p (t d) -> p t d", t=TT)
        facc = O
        rest = top[0]

        win = take(3 * CW).rearrange("p (s k n) -> p s k n", s=3, k=KT)
        bias = take(2 * BX * GRID).rearrange("p (h x c) -> p h x c", h=2, x=BX)
        qna = [take(TOK) for _ in range(2)]
        kna = take(TOK + CTX)
        qdfm = [take(TOK) for _ in range(2)]
        kdf = take(TOK + CTX)
        V = take((TT + 1) * 256).rearrange("p (t n) -> p t n", t=TT + 1)
        Pb = take(4 * 640).rearrange("p (b n) -> p b n", b=4)
        PT = take(2 * 640).rearrange("p (b n) -> p b n", b=2)
        qdf = PT[:, 0, :]
        kout = take(256)
        top[0] = rest
        tables = take(2 * GROUPS * BX * GRID).rearrange("p (h x c) -> p h x c", h=2 * GROUPS, x=BX)
        mask = take(GRID)
        colhot = take(P)
        rpbT = take(P)
        lam_in = take(4 * HD).rearrange("p (m d) -> p m d", m=4)
        lam_tmp = take(HD)
        silu_w = take(KT * CAPW).rearrange("p (k v) -> p k v", k=KT)

        top[0] = rest
        selL = take(4 * E * CAP_L).rearrange("p (t e s) -> p t e s", t=4, e=E)
        selC = take(E * CAP_C).rearrange("p (e s) -> p e s", e=E)
        aff = take(TT * E).rearrange("p (t e) -> p t e", t=TT)
        selGC = take(E * CAP_C)
        GTc = take(2 * P).rearrange("p (a t) -> p a t", a=2)
        lnG = take(D)
        lnB = take(D)
        rest2 = top[0]
        G1 = take(2 * D).rearrange("p (v d) -> p v d", v=2)
        OT = take(D).rearrange("p (k t) -> p k t", k=KT)
        h2T = take(D).rearrange("p (k t) -> p k t", k=KT)
        amax = take(TT)
        asum = take(TT)
        affT = take(TOK)
        work = take(TOK)
        picked = take(TOK)
        rank = take(TOK)
        zeros = take(TOK)
        top8 = take(8)
        pos = take(TT * E).rearrange("p (t e) -> p t e", t=TT)
        scr = take(D)
        top[0] = rest2
        selG = take(4 * 2 * CAP_L).rearrange("p (t e s) -> p t e s", t=4, e=2)
        GT = take(LAT)
        XT = take(KT * 2 * CAPW).rearrange("p (k e s) -> p k e s", k=KT, e=2)
        H = take(2 * FT * CAPW).rearrange("p (e f s) -> p e f s", e=2, f=FT)
        YT = take(KT * P).rearrange("p (k s) -> p k s", k=KT)
        YcT = take(KT * E * CAP_C).rearrange("p (k s) -> p k s", k=KT)
        Y = take(D)
        sg = take(2 * FPC * CAPW).rearrange("p (b f s) -> p b f s", b=2, f=FPC)

        def weights(slot):
            return ring[:, slot, :].rearrange("p (k n) -> p k n", k=KT)

        const_landed = sem("const_landed")
        tokens_landed = sem("tokens_landed")
        landed = [sem(f"chunk_landed{i}") for i in range(RING)]
        chunk_used = sem("chunk_used")
        dve_own = Tally(sem("dve_own"))

        def chunk_source(n):
            if n < ADA_CHUNKS:
                return a["w_ada"][n]
            return a["w_out"][n - ADA_CHUNKS]

        def issue(eng, n):
            if n >= RING:
                eng.wait_ge(chunk_used, n - RING + 1)
            src = chunk_source(n) if n < FIRST_EXPERT_CHUNK else a["w_exp"][n - FIRST_EXPERT_CHUNK]
            eng.dma_start(ring[:, n % RING, :], src).then_inc(landed[n % RING], 16)

        def arrived(eng, n):
            eng.wait_ge(landed[n % RING], 16 * (n // RING + 1))

        def chain(ins):
            ins.then_inc(dve_own.sem, 1)
            dve_own.k += 1
            nc.vector.wait_ge(dve_own.sem, dve_own.value())

        def layer_norm(eng, x, var_sem, std_sem, t):
            for c in range(2):
                chain(eng.bn_stats(bnst[:, c, :], x[:, c * 512:(c + 1) * 512]))
            chain(eng.bn_aggr(bnag[:, 0:2], bnst))
            eng.tensor_scalar(bnag[:, 1:2], bnag[:, 1:2], EPS, None, ALU.add).then_inc(var_sem, 1)
            eng.wait_ge(std_sem, t + 1)
            chain(eng.reciprocal(bnag[:, 3:4], bnag[:, 2:3]))
            chain(eng.tensor_scalar(x, x, bnag[:, 0:1], bnag[:, 3:4], ALU.subtract, ALU.mult))

        v_ready = sem("v_ready")
        negmax_ready = sem("negmax_ready")
        o_ready = sem("o_ready")
        p_ready = sem("p_ready")
        pt_copied = sem("pt_copied")
        o_done = sem("o_done")
        k_stored = sem("k_stored")
        v_stored = sem("v_stored")
        scat_ready = sem("scat_ready")
        scat_added = sem("scat_added")

        silu_done = sem("silu_done")
        mod_done = sem("mod_done")
        tab_ready = sem("tab_ready")
        tab_copied = sem("tab_copied")
        tab_stored = sem("tab_stored")
        ada_added = sem("ada_added")
        wide_zero = sem("wide_zero")
        rpb_zero = sem("rpb_zero")
        gates_stored = sem("gates_stored")
        h_done = sem("h_done")
        CK = 4
        HR = P
        CONSTS = [(ident, "ident"), (rotM, "rotM"), (cosT, "cosT"), (sinT, "sinT"), (mask, "mask"),
                  (iota1, "iota1"), (silu_c, "cvecs"), (badaT, "b_ada"), (wroute, "w_router")]
        n_const = len(CONSTS) + 4

        with nc.Block() as block:
            @block.sync
            def _(eng):
                for primed in (v_ready, negmax_ready, o_ready, p_ready, pt_copied, o_done, k_stored, v_stored,
                               scat_ready, scat_added):
                    eng.sem_inc(primed, PRIMED)
                for dst, name in CONSTS:
                    eng.dma_start(dst, a[name]).then_inc(const_landed, 16)
                eng.dma_start(colhot[0:DC], a["colhot"]).then_inc(const_landed, 16)
                eng.wait_ge(rpb_zero, 1)
                eng.dma_start(rpbT[0:DC, 0:2 * GROUPS * DR], a["rpbT"].rearrange("c h r -> c (h r)")).then_inc(const_landed, 16)
                eng.dma_start(lam_in, a["lambdas"].partition_broadcast(P)).then_inc(const_landed, 16)
                eng.dma_start(subg, a["subln_g"].partition_broadcast(P)).then_inc(const_landed, 16)
                for n in range(RING):
                    issue(eng, n)
                eng.dma_start(xT, a["xT"]).then_inc(tokens_landed, 16)
                for n in range(RING, ADA_CHUNKS + RING):
                    issue(eng, n)

            @block.gpsimd
            def _(eng):
                eng.memset(rpbT, 0.0).then_inc(rpb_zero, 1)
                eng.wait_ge(tab_copied, 2 * GRID // CK)
                for g in range(GROUPS):
                    eng.dma_start(bias_scratch[g], tables[:, 2 * g:2 * g + 2].rearrange("p h x c -> p (h x c)")
                                  ).then_inc(tab_stored, 16)
                eng.wait_ge(mod_done, 1)
                with nc.allow_non_contiguous_dma(reason="8 KiB turned from columns into rows"):
                    for v in range(2):
                        for k in range(KT):
                            eng.dma_start(gate_scratch[v, k].unsqueeze(1), modT[:, 2, k, v:v + 1]
                                          ).then_inc(gates_stored, 16)
                eng.wait_ge(gates_stored, 16 * 2 * KT)
                eng.wait_ge(tab_stored, 16 * GROUPS)

            @block.scalar
            def _(eng):
                eng.wait_ge(const_landed, 16 * n_const)
                eng.wait_ge(wide_zero, 1)
                eng.activation(silu_w[:, :, 0:2], silu_c, ACT.Silu).then_inc(silu_done, 1)
                eng.wait_ge(mod_done, 1)
                eng.wait_ge(tokens_landed, 16)
                for k in range(0, KT, 2):
                    for v, t0, t1 in ((0, 0, CTX), (1, CTX, TOK)):
                        eng.activation(xT[:, k, t0:t1], xT[:, k, t0:t1], ACT.Identity,
                                       bias=modT[:, 0, k, v:v + 1], scale=modT[:, 1, k, v:v + 1]
                                       ).then_inc(h_done, 1)

            @block.tensor
            def _(eng):
                eng.wait_ge(const_landed, 16 * n_const)
                for b in range(GRID // CK):
                    if b >= 4:
                        eng.wait_ge(tab_copied, 2 * (b - 3))
                    for c in range(CK):
                        s = GRID - (b * CK + c)
                        for half in range(2):
                            mm = eng.matmul(ps[64 * half:64 * half + 64, b % 4, c * HR:(c + 1) * HR],
                                            colhot[0:DC, s:s + GRID], rpbT[0:DC, :], start=True, stop=True)
                    mm.then_inc(tab_ready, 1)
                eng.wait_ge(silu_done, 1)
                for n in range(ADA_CHUNKS):
                    arrived(eng, n)
                    if n >= 4:
                        eng.wait_ge(ada_added, n - 3)
                    w = weights(n % RING)
                    for j in range(2):
                        for k in range(KT):
                            mm = eng.matmul(ps[:, 4 + n % 4, j * CAPW:(j + 1) * CAPW], w[:, k, j * P:(j + 1) * P],
                                            silu_w[:, k, :], start=(k == 0), stop=(k == KT - 1))
                    mm.then_inc(chunk_used, 1)

            @block.vector
            def _(eng):
                eng.wait_ge(const_landed, 16 * n_const)
                eng.memset(silu_w.rearrange("p k v -> p (k v)"), 0.0).then_inc(wide_zero, 1)
                chain(eng.memset(tables.rearrange("p h x c -> p (h x c)"), 0.0))
                for b in range(GRID // CK):
                    eng.wait_ge(tab_ready, b + 1)
                    for half in range(2):
                        p0 = 64 * half
                        src = ps[p0:p0 + 64, b % 4, :].rearrange("p (c n) -> p c n", c=CK)[:, :, 0:2 * GROUPS * DR]
                        dst = tables[p0:p0 + 64, :, half:half + DR, b * CK:(b + 1) * CK]
                        m = mask[p0:p0 + 64, b * CK:(b + 1) * CK].unsqueeze(1).unsqueeze(1)
                        eng.tensor_tensor(dst, src.rearrange("p c (h r) -> p h r c", r=DR),
                                          m.broadcast_to([64, 2 * GROUPS, DR, CK]), ALU.add).then_inc(tab_copied, 1)
                for m in range(2):
                    chain(eng.tensor_tensor_reduce(lam_tmp, lam_in[:, 2 * m, :], lam_in[:, 2 * m + 1, :], 1.0, 0.0,
                                                   ALU.mult, ALU.add, lam_s[:, m:m + 1]))
                flat, b_flat = modT.rearrange("p m k v -> p (m k) v"), badaT.rearrange("p m k -> p (m k)")
                for n in range(ADA_CHUNKS):
                    eng.wait_ge(chunk_used, n + 1)
                    src = ps[:, 4 + n % 4, 0:2 * CAPW].rearrange("p (j c) -> p j c", j=2)[:, :, 0:2]
                    eng.tensor_tensor(flat[:, 2 * n:2 * n + 2, :], src,
                                      b_flat[:, 2 * n:2 * n + 2].unsqueeze(2).broadcast_to([P, 2, 2]), ALU.add
                                      ).then_inc(ada_added, 1)
                eng.wait_ge(ada_added, ADA_CHUNKS)
                for m in (1, 4):
                    ins = eng.tensor_scalar(modT[:, m], modT[:, m], 1.0, None, ALU.add)
                    if m == 1:
                        chain(ins)
                ins.then_inc(mod_done, 1)
                eng.wait_ge(mod_done, 1)
                eng.wait_ge(tokens_landed, 16)
                for k in range(1, KT, 2):
                    for v, t0, t1 in ((0, 0, CTX), (1, CTX, TOK)):
                        eng.tensor_scalar(xT[:, k, t0:t1], xT[:, k, t0:t1], modT[:, 1, k, v:v + 1],
                                          modT[:, 0, k, v:v + 1], ALU.mult, ALU.add).then_inc(h_done, 1)

        U, S_STEPS = units()
        NU = len(U)
        win_landed = [sem(f"win_landed{i}") for i in range(3)]
        bias_landed = sem("bias_landed")
        cache_landed = sem("cache_landed")
        qk_ready = sem("qk_ready")
        qk_copied = sem("qk_copied")
        v_copied = sem("v_copied")
        rot_ready = sem("rot_ready")
        rope_done = sem("rope_done")
        kctx_ready = sem("kctx_ready")
        kctx_copied = sem("kctx_copied")
        s_ready = sem("s_ready")
        a_ready = sem("a_ready")
        pt_ready = sem("pt_ready")
        lam_exp = sem("lam_exp")
        q_zero = sem("q_zero")

        with nc.Block() as block:
            @block.sync
            def _(eng):
                with eng.Fori(0, GROUPS) as i:
                    eng.wait_ge(v_ready, i * TT + PRIMED)
                    for s in range(3):
                        eng.dma_start(win[:, s], a["w_in"][i, s]).then_inc(win_landed[s], 16)
                    eng.wait_ge(negmax_ready, i * S_STEPS + PRIMED)
                    eng.dma_start(bias.rearrange("p h x c -> p (h x c)"), bias_scratch[i]).then_inc(bias_landed, 16)
                    eng.wait_ge(o_ready, i * NU + PRIMED)
                    eng.dma_start(kna[:, TOK:], a["cacheKT"][i, 0]).then_inc(cache_landed, 16)
                    eng.dma_start(kdf[:, TOK:], a["cacheKT"][i, 1]).then_inc(cache_landed, 16)
                    eng.dma_start(V[:, TT, :], a["cacheV"][i]).then_inc(cache_landed, 16)
                    eng.wait_ge(v_copied, i * TT + 1)
                    eng.dma_start(a["v_new"][i], V[:, 0, :]).then_inc(v_stored, 16)
                    eng.wait_ge(kctx_copied, i + 1)
                    eng.dma_start(a["k_new"][i], kout).then_inc(k_stored, 16)
                eng.wait_ge(v_stored, 16 * GROUPS + PRIMED)
                eng.wait_ge(k_stored, 16 * GROUPS + PRIMED)

            @block.tensor
            def _(eng):
                eng.wait_ge(h_done, 2 * KT)
                with eng.Fori(0, GROUPS) as i:
                    eng.wait_ge(p_ready, i * S_STEPS + PRIMED)
                    eng.wait_ge(pt_copied, i * NU + PRIMED)
                    eng.wait_ge(o_done, i * NU + PRIMED)
                    for g in range(4):
                        if g % 2 == 0:
                            eng.wait_ge(win_landed[g // 2], i * 16 + 16)
                        w = win[:, g // 2]
                        for bank, t0, t1 in ((2 * g, CTX, TOK), (2 * g + 1, 0, CTX)):
                            for k in range(KT):
                                mm = eng.matmul(ps[:, bank, 0:t1 - t0], w[:, k, (g % 2) * P:(g % 2 + 1) * P],
                                                xT[:, k, t0:t1], start=(k == 0), stop=(k == KT - 1))
                        mm.then_inc(qk_ready, 1)
                    eng.wait_ge(win_landed[2], i * 16 + 16)
                    for t in range(TT):
                        eng.wait_ge(qk_copied, i * 4 + t // 2 + 1)
                        for k in range(KT):
                            mm = eng.matmul(ps[:, t, 0:256], xT[:, k, t * P:(t + 1) * P], win[:, 2, k, :],
                                            start=(k == 0), stop=(k == KT - 1))
                        mm.then_inc(v_ready, 1)
                    eng.wait_ge(qk_copied, i * 4 + 4)
                    for n, src in enumerate((qdf, kdf)):
                        eng.matmul(ps[:, 5 + n, :], rotM, src[:, CTX:TOK], start=True, stop=True
                                   ).then_inc(rot_ready, 1)
                    for n, src in enumerate((kna, kdf)):
                        mm = eng.transpose(ps[:, 7, n * P:(n + 1) * P], src[:, 0:CTX], ident)
                    mm.then_inc(kctx_ready, 1)
                    eng.wait_ge(v_copied, i * TT + TT)
                    eng.wait_ge(kctx_copied, i + 1)
                    eng.wait_ge(rope_done, i * 2 + 2)
                    eng.wait_ge(cache_landed, i * 48 + 48)

                    def scores(u):
                        kind, h, t, n, steps = U[u]
                        for m, s in enumerate(steps):
                            q, kk = (qna[h], kna) if kind == "na" else (qdfm[m], kdf)
                            if s >= 2:
                                eng.wait_ge(p_ready, i * S_STEPS + (s - 1) + PRIMED)
                            b = 2 * (s % 2)
                            lhs = q[:, t * P:(t + 1) * P]
                            if t == 0:
                                mm = eng.matmul(ps[:, b, 0:CTX], lhs, kk[:, 0:CTX], start=True, stop=True)
                            else:
                                eng.matmul(ps[:, b, 0:LAT], lhs, kk[:, CTX:TOK], start=True, stop=True)
                                mm = eng.matmul(ps[:, b + 1, 0:CTX], lhs, kk[:, TOK:], start=True, stop=True)
                            mm.then_inc(s_ready, 1)

                    def turn(u):
                        kind, h, t, n, steps = U[u]
                        if kind == "na":
                            eng.wait_ge(p_ready, i * S_STEPS + steps[0] + 1 + PRIMED)
                        else:
                            eng.wait_ge(a_ready, i * TT + t + 1)
                        if u >= 1:
                            eng.wait_ge(pt_copied, i * NU + u + PRIMED)
                        for c in range(n // P):
                            mm = eng.transpose(ps[:, 4 + c // 4, (c % 4) * P:(c % 4 + 1) * P],
                                               Pb[:, steps[0] % 4, c * P:(c + 1) * P], ident)
                        mm.then_inc(pt_ready, 1)

                    def weigh(u):
                        kind, h, t, n, steps = U[u]
                        eng.wait_ge(pt_copied, i * NU + u + 1 + PRIMED)
                        if u >= 2:
                            eng.wait_ge(o_done, i * NU + u - 1 + PRIMED)
                        c0, c1 = (0, P) if kind == "na" else (P, 2 * P)
                        for c in range(n // P):
                            mm = eng.matmul(ps[:, 6 + u % 2, 0:c1 - c0], PT[:, u % 2, c * P:(c + 1) * P],
                                            V[:, c + 1 if t else 0, c0:c1], start=(c == 0), stop=(c == n // P - 1))
                        mm.then_inc(o_ready, 1)

                    for k in range(NU + 2):
                        if k < NU:
                            scores(k)
                        if 1 <= k <= NU:
                            turn(k - 1)
                        if k >= 2:
                            weigh(k - 2)

            @block.scalar
            def _(eng):
                eng.wait_ge(q_zero, 4)
                for m in range(2):
                    ins = eng.activation(lam_s[:, 2 + m:3 + m], lam_s[:, m:m + 1], ACT.Exp)
                ins.then_inc(lam_exp, 1)
                with eng.Fori(0, GROUPS) as i:
                    for g, dst in enumerate((None, kna, qdf, kdf)):
                        eng.wait_ge(qk_ready, i * 4 + g + 1)
                        sc = SCALE if g % 2 == 0 else 1.0
                        parts = [(0, P, dst)] if g else [(0, 64, qna[0]), (64, P, qna[1])]
                        for p0, p1, x in parts:
                            eng.activation(x[p0:p1, CTX:TOK], ps[p0:p1, 2 * g, :], ACT.Copy, scale=sc)
                            ins = eng.activation(x[p0:p1, 0:CTX], ps[p0:p1, 2 * g + 1, 0:CTX], ACT.Copy, scale=sc)
                        ins.then_inc(qk_copied, 1)
                    eng.wait_ge(kctx_ready, i + 1)
                    eng.wait_ge(k_stored, i * 16 + PRIMED)
                    eng.activation(kout, ps[:, 7, 0:256], ACT.Copy).then_inc(kctx_copied, 1)

                    def exps(u):
                        kind, h, t, n, steps = U[u]
                        for s in steps:
                            eng.wait_ge(negmax_ready, i * S_STEPS + s + 1 + PRIMED)
                            if s >= 4:
                                user = [w for w in range(NU) if s - 4 in U[w][4]][0]
                                eng.wait_ge(pt_ready, i * NU + user + 1)
                            b = 2 * (s % 2)
                            src = ps[:, b:b + 2, :].rearrange("p b n -> p (b n)")[:, 0:n]
                            eng.activation(Pb[:, s % 4, 0:n], src, ACT.Exp, bias=stat[:, s, 2:3], scale=1.0,
                                           accum_out=stat[:, s, 3:4]).then_inc(p_ready, 1)

                    def copy_turned(u):
                        kind, h, t, n, steps = U[u]
                        eng.wait_ge(pt_ready, i * NU + u + 1)
                        eng.wait_ge(o_ready, i * NU + max(u - 1, 0) + PRIMED)
                        src = ps[:, 4:6, :].rearrange("p b n -> p (b n)")[:, 0:n]
                        eng.activation(PT[:, u % 2, 0:n], src, ACT.Copy).then_inc(pt_copied, 1)

                    for k in range(NU + 1):
                        if k < NU:
                            exps(k)
                        if k >= 1:
                            copy_turned(k - 1)

            @block.vector
            def _(eng):
                for x in (*qna, *qdfm):
                    eng.memset(x, 0.0).then_inc(q_zero, 1)
                eng.wait_ge(lam_exp, 1)
                chain(eng.tensor_tensor(lam_s[:, 4:5], lam_s[:, 3:4], lam_s[:, 2:3], ALU.subtract))
                chain(eng.tensor_scalar(lam_s[:, 4:5], lam_s[:, 4:5], -LAMBDA_INIT, None, ALU.add))
                with eng.Fori(0, GROUPS) as i:
                    dve_own.enter(i, 4 + 2 * (TT - 1) + 2 * TT + 3 * TT)
                    for t in range(TT):
                        if t == 0:
                            eng.wait_ge(v_stored, i * 16 + PRIMED)
                        eng.wait_ge(v_ready, i * TT + t + 1 + PRIMED)
                        eng.tensor_copy(V[:, t, :], ps[:, t, 0:256]).then_inc(v_copied, 1)
                    for n, x in enumerate((qdf, kdf)):
                        eng.wait_ge(rot_ready, i * 2 + n + 1)
                        lat = x[:, CTX:TOK]
                        tmp = Pb[:, n, 0:LAT]
                        eng.wait_ge(qk_copied, i * 4 + 3 + n)
                        chain(eng.tensor_tensor(tmp, ps[:, 5 + n, :], sinT, ALU.mult))
                        chain(eng.tensor_tensor(lat, lat, cosT, ALU.mult))
                        if n == 0:
                            for p0, x2 in ((0, qdfm[0]), (64, qdfm[1])):
                                eng.tensor_copy(x2[p0:p0 + 64, 0:CTX], x[p0:p0 + 64, 0:CTX])
                                ins = eng.tensor_tensor(x2[p0:p0 + 64, CTX:TOK], lat[p0:p0 + 64], tmp[p0:p0 + 64], ALU.add)
                            ins.then_inc(rope_done, 1)
                        else:
                            eng.tensor_tensor(lat, lat, tmp, ALU.add).then_inc(rope_done, 1)

                    def maxima(u):
                        kind, h, t, n, steps = U[u]
                        for s in steps:
                            eng.wait_ge(s_ready, i * S_STEPS + s + 1)
                            b = 2 * (s % 2)
                            src = ps[:, b:b + 2, :].rearrange("p b n -> p (b n)")
                            if kind == "na" and t:
                                if s == 1:
                                    eng.wait_ge(bias_landed, i * 16 + 16)
                                x0 = DR - ROWS - 2 * (t - 1)
                                table = bias[:, h, x0:x0 + ROWS, :].rearrange("p x c -> p (x c)")
                                eng.tensor_reduce(stat[:, s, 1:2], src[:, LAT:n], AX_X, ALU.max)
                                chain(eng.tensor_tensor_reduce(src[:, 0:LAT], src[:, 0:LAT], table, 1.0, -3e38, ALU.add,
                                                               ALU.max, stat[:, s, 0:1]))
                                eng.tensor_reduce(stat[:, s, 2:3], stat[:, s, 0:2], AX_X, ALU.max,
                                                  negate=True).then_inc(negmax_ready, 1)
                            else:
                                eng.tensor_reduce(stat[:, s, 2:3], src[:, 0:n], AX_X, ALU.max,
                                                  negate=True).then_inc(negmax_ready, 1)

                    def combine(u):
                        kind, h, t, n, steps = U[u]
                        s0, s1 = steps[0], steps[-1]
                        eng.wait_ge(p_ready, i * S_STEPS + s1 + 1 + PRIMED)
                        chain(eng.reciprocal(rec[:, u, 0:1], stat[:, s0, 3:4]))
                        if kind == "df":
                            chain(eng.reciprocal(rec[:, u, 1:2], stat[:, s1, 3:4]))
                            chain(eng.tensor_scalar(rec[:, u, 1:2], rec[:, u, 1:2], stat[:, s0, 3:4], lam_s[:, 4:5],
                                                    ALU.mult, ALU.mult))
                            eng.scalar_tensor_tensor(out=Pb[:, s0 % 4, 0:n], in0=Pb[:, s1 % 4, 0:n],
                                                     scalar=rec[:, u, 1:2], in1=Pb[:, s0 % 4, 0:n],
                                                     op0=ALU.mult, op1=ALU.add).then_inc(a_ready, 1)

                    def outputs(u):
                        kind, h, t, n, steps = U[u]
                        eng.wait_ge(o_ready, i * NU + u + 1 + PRIMED)
                        w = HD if kind == "na" else 2 * HD
                        off = 64 * h if kind == "na" else LAT
                        eng.tensor_scalar(O[:, t, bass.ds(i * P + off, w)], ps[:, 6 + u % 2, h * HD:h * HD + w], rec[:, u, 0:1],
                                          None, ALU.mult).then_inc(o_done, 1)

                    for k in range(NU + 2):
                        if k < NU:
                            maxima(k)
                        if 1 <= k <= NU:
                            combine(k - 1)
                        if k >= 2:
                            outputs(k - 2)
                dve_own.leave(GROUPS)

        route_landed = sem("route_landed")
        rms_sq = sem("rms_sq")
        rms_rt = sem("rms_rt")
        o_scaled = sem("o_scaled")
        ot_ready = sem("ot_ready")
        ot_copied = sem("ot_copied")
        proj_ready = sem("proj_ready")
        proj_done = sem("proj_done")
        var_ready = sem("var_ready")
        std_ready = sem("std_ready")
        x1_done = sem("x1_done")
        xt_ready = sem("xt_ready")
        h2_done = sem("h2_done")
        logit_ready = sem("logit_ready")
        logit_sub = sem("logit_sub")
        aff_exp = sem("aff_exp")
        aff_done = sem("aff_done")
        afft_ready = sem("afft_ready")
        rank_done = sem("rank_done")
        pos_ready = sem("pos_ready")
        sel_done = sem("sel_done")
        gtc_ready = sem("gtc_ready")
        gtc_copied = sem("gtc_copied")
        NT = TT * GROUPS

        with nc.Block() as block:
            @block.sync
            def _(eng):
                eng.dma_start(x1, a["x"].rearrange("t p d -> p t d")).then_inc(route_landed, 16)
                eng.dma_start(G1, gate_scratch.rearrange("v k p -> v (k p)").partition_broadcast(P)).then_inc(route_landed, 16)
                eng.dma_start(lnG, a["ln1_g"].partition_broadcast(P)).then_inc(route_landed, 16)
                eng.dma_start(lnB, a["ln1_b"].partition_broadcast(P)).then_inc(route_landed, 16)
                for n in range(ADA_CHUNKS + RING, ADA_CHUNKS + RING + OUT_CHUNKS):
                    issue(eng, n)
                eng.wait_ge(x1_done, TT)
                eng.dma_start(lnG, a["ln2_g"].partition_broadcast(P)).then_inc(route_landed, 16)
                eng.dma_start(lnB, a["ln2_b"].partition_broadcast(P)).then_inc(route_landed, 16)

            @block.tensor
            def _(eng):
                for t in range(TT):
                    eng.wait_ge(o_scaled, t + 1)
                    if t >= 1:
                        eng.wait_ge(ot_copied, t)
                    for k in range(KT):
                        mm = eng.transpose(ps[:, k // 4, (k % 4) * P:(k % 4 + 1) * P], O[:, t, k * P:(k + 1) * P], ident)
                    mm.then_inc(ot_ready, 1)
                    eng.wait_ge(ot_copied, t + 1)
                    if t >= 1:
                        eng.wait_ge(proj_done, t)
                    for c in range(OUT_CHUNKS):
                        n = ADA_CHUNKS + c
                        if t == 0:
                            arrived(eng, n)
                        for k in range(KT):
                            mm = eng.matmul(ps[:, 2 + c // 2, (c % 2) * 256:(c % 2 + 1) * 256], OT[:, k, :],
                                            weights(n % RING)[:, k, :], start=(k == 0), stop=(k == KT - 1))
                        if t == TT - 1:
                            mm.then_inc(chunk_used, 1)
                    if t < TT - 1:
                        mm.then_inc(proj_ready, 1)
                for t in range(TT):
                    eng.wait_ge(x1_done, t + 1)
                    if t >= 1:
                        eng.wait_ge(h2_done, t)
                    for k in range(KT):
                        mm = eng.transpose(ps[:, 4 + k // 4, (k % 4) * P:(k % 4 + 1) * P], x1[:, t, k * P:(k + 1) * P], ident)
                    mm.then_inc(xt_ready, 1)
                    eng.wait_ge(h2_done, t + 1)
                    for k in range(KT):
                        mm = eng.matmul(ps[:, 7, t * E:(t + 1) * E], h2T[:, k, :], wroute[:, k, :],
                                        start=(k == 0), stop=(k == KT - 1))
                    mm.then_inc(logit_ready, 1)
                eng.wait_ge(aff_done, 1)
                for t in range(TT):
                    mm = eng.transpose(ps[0:E, t // 4, (t % 4) * P:(t % 4 + 1) * P], aff[:, t, :], ident)
                mm.then_inc(afft_ready, 1)
                eng.wait_ge(rank_done, 1)
                for t in range(TT):
                    mm = eng.transpose(ps[:, 2, t * E:(t + 1) * E], rank[0:E, t * P:(t + 1) * P], ident[0:E, 0:E])
                mm.then_inc(pos_ready, 1)
                eng.wait_ge(sel_done, 1)
                for c in range(2):
                    mm = eng.transpose(ps[:, 3, c * P:(c + 1) * P], selGC[:, c * P:(c + 1) * P], ident)
                mm.then_inc(gtc_ready, 1)

            @block.scalar
            def _(eng):
                eng.wait_ge(rms_sq, 1)
                eng.activation(rms[:, 1, :], rms[:, 0, :], ACT.Sqrt).then_inc(rms_rt, 1)
                for t in range(TT):
                    eng.wait_ge(ot_ready, t + 1)
                    if t >= 1:
                        eng.wait_ge(proj_ready, t)
                    eng.activation(OT.rearrange("p k t -> p (k t)"), ps[:, 0:2, :].rearrange("p b n -> p (b n)"),
                                   ACT.Copy).then_inc(ot_copied, 1)
                    eng.wait_ge(var_ready, t + 1)
                    eng.activation(bnag[:, 2:3], bnag[:, 1:2], ACT.Sqrt).then_inc(std_ready, 1)
                for t in range(TT):
                    eng.wait_ge(xt_ready, t + 1)
                    if t >= 1:
                        eng.wait_ge(logit_ready, t)
                    v = min(t, 1)
                    for k in range(KT):
                        ins = eng.activation(h2T[:, k, :], ps[:, 4 + k // 4, (k % 4) * P:(k % 4 + 1) * P], ACT.Identity,
                                             bias=modT[:, 3, k, v:v + 1], scale=modT[:, 4, k, v:v + 1])
                    ins.then_inc(h2_done, 1)
                eng.wait_ge(logit_sub, 1)
                eng.activation(aff, aff, ACT.Exp).then_inc(aff_exp, 1)
                eng.wait_ge(gtc_ready, 1)
                eng.activation(GTc.rearrange("p a t -> p (a t)"), ps[:, 3, 0:256], ACT.Copy).then_inc(gtc_copied, 1)

            @block.vector
            def _(eng):
                n = 0
                for t in range(TT):
                    for h in range(GROUPS):
                        part = O[:, t, LAT + h * P:LAT + (h + 1) * P]
                        ins = eng.tensor_tensor_reduce(scr[:, 0:P], part, part, 1.0 / P, EPS, ALU.mult, ALU.add,
                                                       rms[:, 0, n:n + 1])
                        n += 1
                        if n < TT * GROUPS:
                            chain(ins)
                ins.then_inc(rms_sq, 1)
                eng.wait_ge(rms_rt, 1)
                chain(eng.reciprocal(rms[:, 2, :], rms[:, 1, :]))
                chain(eng.tensor_scalar(subg, subg, 1.0 - LAMBDA_INIT, None, ALU.mult))
                n = 0
                for t in range(TT):
                    for h in range(GROUPS):
                        part = O[:, t, LAT + h * P:LAT + (h + 1) * P]
                        ins = eng.scalar_tensor_tensor(out=part, in0=part, scalar=rms[:, 2, n:n + 1], in1=subg,
                                                       op0=ALU.mult, op1=ALU.mult)
                        n += 1
                    ins.then_inc(o_scaled, 1)
                eng.wait_ge(route_landed, 16 * 4)
                for t in range(TT):
                    v = min(t, 1)
                    if t < TT - 1:
                        eng.wait_ge(proj_ready, t + 1)
                    else:
                        eng.wait_ge(chunk_used, ADA_CHUNKS + OUT_CHUNKS)
                    eng.tensor_tensor(scr, ps[:, 2:4, :].rearrange("p b n -> p (b n)"), G1[:, v, :], ALU.mult
                                      ).then_inc(proj_done, 1)
                    eng.wait_ge(proj_done, t + 1)
                    ins = eng.scalar_tensor_tensor(out=x1[:, t, :], in0=x1[:, t, :], scalar=ALPHA, in1=scr,
                                                   op0=ALU.mult, op1=ALU.add)
                    chain(ins)
                    layer_norm(eng, x1[:, t, :], var_ready, std_ready, t)
                    chain(eng.tensor_tensor(x1[:, t, :], x1[:, t, :], lnG, ALU.mult))
                    eng.tensor_tensor(x1[:, t, :], x1[:, t, :], lnB, ALU.add).then_inc(x1_done, 1)
                eng.wait_ge(logit_ready, TT)
                logits = ps[:, 7, 0:TT * E].rearrange("p (t e) -> p t e", t=TT)
                chain(eng.tensor_reduce(amax, logits, AX_X, ALU.max))
                eng.tensor_tensor(aff, logits, amax.unsqueeze(2).broadcast_to([P, TT, E]), ALU.subtract
                                  ).then_inc(logit_sub, 1)
                eng.wait_ge(aff_exp, 1)
                chain(eng.tensor_reduce(asum, aff, AX_X, ALU.add))
                chain(eng.reciprocal(asum, asum))
                eng.tensor_tensor(aff, aff, asum.unsqueeze(2).broadcast_to([P, TT, E]), ALU.mult
                                  ).then_inc(aff_done, 1)
                eng.wait_ge(afft_ready, 1)
                chain(eng.tensor_copy(affT[0:E, 0:LAT], ps[0:E, 0, :]))
                chain(eng.tensor_copy(affT[0:E, LAT:TOK], ps[0:E, 1, 0:P]))
                for t0, t1, cap in ((0, CTX, CAP_C), (CTX, TOK, CAP_L)):
                    w = affT[0:E, t0:t1]
                    for r in range(cap // 8):
                        chain(eng.max(top8[0:E], w))
                        chain(eng.match_replace(w, top8[0:E], w, -1.0))
                chain(eng.memset(zeros[0:E], 0.0))
                chain(eng.tensor_scalar(picked[0:E], affT[0:E], 0.0, None, ALU.is_lt))
                for t0, t1 in ((0, CTX), (CTX, TOK)):
                    chain(eng.tensor_tensor_scan(work[0:E, t0:t1], picked[0:E, t0:t1], zeros[0:E, t0:t1], 0.0,
                                                 ALU.add, ALU.add))
                eng.tensor_tensor(rank[0:E], work[0:E], picked[0:E], ALU.mult).then_inc(rank_done, 1)
                eng.wait_ge(pos_ready, 1)
                chain(eng.tensor_copy(pos, ps[:, 2, 0:TT * E].rearrange("p (t e) -> p t e", t=TT)))
                for t in range(1, TT):
                    eng.tensor_tensor(selL[:, t - 1], pos[:, t, :].unsqueeze(2).broadcast_to([P, E, CAP_L]),
                                      iota1.unsqueeze(1).broadcast_to([P, E, CAP_L]), ALU.is_equal)
                chain(eng.tensor_tensor(selC, pos[:, 0, :].unsqueeze(2).broadcast_to([P, E, CAP_C]),
                                        iota1[:, 0:CAP_C].unsqueeze(1).broadcast_to([P, E, CAP_C]), ALU.is_equal))
                eng.tensor_tensor(selGC.rearrange("p (e s) -> p e s", e=E), selC,
                                  aff[:, 0, :].unsqueeze(2).broadcast_to([P, E, CAP_C]), ALU.mult
                                  ).then_inc(sel_done, 1)

        gather_ready = sem("gather_ready")
        gather_done = sem("gather_done")
        selg_done = sem("selg_done")
        gt_ready = sem("gt_ready")
        gt_copied = sem("gt_copied")
        silu_ready = sem("silu_ready")
        h_ready = sem("h_ready")
        yt_done = sem("yt_done")
        y_ready = sem("y_ready")
        y_copied = sem("y_copied")
        acc_zero = sem("acc_zero")
        C2 = 2 * NC_F

        with nc.Block() as block:
            @block.sync
            def _(eng):
                first = ADA_CHUNKS + OUT_CHUNKS + RING
                rounds = (FIRST_EXPERT_CHUNK + EXPERT_CHUNKS - first) // RING
                assert first + rounds * RING == FIRST_EXPERT_CHUNK + EXPERT_CHUNKS
                with eng.Fori(0, rounds) as r:
                    for m in range(RING):
                        n = first + m
                        eng.wait_ge(chunk_used, r * RING + (n - RING + 1))
                        eng.dma_start(ring[:, n % RING, :], a["w_exp"][r * RING + (n - FIRST_EXPERT_CHUNK)]
                                      ).then_inc(landed[n % RING], 16)

            @block.tensor
            def _(eng):
                eng.wait_ge(gtc_copied, 1)
                with eng.Fori(0, PAIRS) as j:
                    for k in range(KT):
                        bank, c0 = k // 3, (k % 3) * 2 * CAP
                        for t in range(1, TT):
                            eng.matmul(ps[:, bank, c0:c0 + 2 * CAP_L], x1[:, t, k * P:(k + 1) * P],
                                       selL[:, t - 1, bass.ds(j * 2, 2), :], start=(t == 1), stop=(t == TT - 1))
                        mm = eng.matmul(ps[:, bank, c0 + 2 * CAP_L:c0 + 2 * CAP], x1[:, 0, k * P:(k + 1) * P],
                                        selC[:, bass.ds(j * 2, 2), :], start=True, stop=True)
                    mm.then_inc(gather_ready, 1)
                    eng.wait_ge(selg_done, j + 1)
                    for t in range(4):
                        mm = eng.transpose(ps[:, 3, t * P:(t + 1) * P], selG[:, t].rearrange("p e s -> p (e s)"), ident)
                    mm.then_inc(gt_ready, 1)
                    eng.wait_ge(gather_done, j * 2 * KT + 2 * KT)
                    for e in range(2):
                        for c in range(NC_F):
                            q = e * NC_F + c
                            if q >= 2:
                                eng.wait_ge(h_ready, j * C2 + q - 1)
                            for w in range(2):
                                m = e * 3 * NC_F + 2 * c + w
                                n = FIRST_EXPERT_CHUNK + m
                                eng.wait_ge(landed[n % RING], j * (16 * PER_PAIR // RING) + 16 * (n // RING + 1))
                                for f in range(FPC):
                                    c0 = (w * FPC + f) * CAPW
                                    for k in range(KT):
                                        mm = eng.matmul(ps[:, q % 2, c0:c0 + CAPW],
                                                        weights(n % RING)[:, k, f * P:(f + 1) * P], XT[:, k, e, :],
                                                        start=(k == 0), stop=(k == KT - 1))
                                mm.then_inc(chunk_used, 1)
                        if e == 1:
                            eng.wait_ge(yt_done, j * 8 + 4)
                        for c in range(NC_F):
                            q = e * NC_F + c
                            m = e * 3 * NC_F + 2 * NC_F + c
                            n = FIRST_EXPERT_CHUNK + m
                            eng.wait_ge(h_ready, j * C2 + q + 1)
                            eng.wait_ge(landed[n % RING], j * (16 * PER_PAIR // RING) + 16 * (n // RING + 1))
                            wd = ring[:, n % RING, :].rearrange("p (f d) -> p f d", f=FPC)
                            for f in range(FPC):
                                ft = c * FPC + f
                                for k in range(KT):
                                    mm = eng.matmul(ps[:, 4 + k // 4, (k % 4) * CAPW:(k % 4 + 1) * CAPW],
                                                    wd[:, f, k * P:(k + 1) * P], H[:, e, ft, :],
                                                    start=(ft == 0 and k % 4 == 0), stop=(ft == FT - 1),
                                                    skip_group_check=True)
                            mm.then_inc(chunk_used, 1)
                    eng.wait_ge(yt_done, j * 8 + 8)
                    eng.wait_ge(scat_added, j * 8 + PRIMED)
                    for k in range(KT):
                        mm = eng.transpose(ps[:, 6 + k // 4, (k % 4) * P:(k % 4 + 1) * P], YT[:, k, :], ident)
                    mm.then_inc(y_ready, 1)
                    eng.wait_ge(y_copied, j + 1)
                    eng.wait_ge(gt_copied, j + 1)
                    for s in range(8):
                        if s >= 2:
                            eng.wait_ge(scat_added, j * 8 + s - 1 + PRIMED)
                        eng.matmul(ps[:, 6 + s % 2, :], GT[:, (s // 2) * P:(s // 2 + 1) * P],
                                   Y[:, (s % 2) * 512:(s % 2 + 1) * 512], start=True, stop=True
                                   ).then_inc(scat_ready, 1)

            @block.scalar
            def _(eng):
                with eng.Fori(0, PAIRS) as j:
                    eng.wait_ge(gt_ready, j + 1)
                    eng.wait_ge(scat_ready, j * 8 + PRIMED)
                    eng.activation(GT, ps[:, 3, :], ACT.Copy).then_inc(gt_copied, 1)
                    for q in range(C2):
                        e, c = q // NC_F, q % NC_F
                        eng.wait_ge(chunk_used, j * PER_PAIR + ADA_CHUNKS + OUT_CHUNKS + e * 3 * NC_F + 2 * c + 2)
                        if q >= 2:
                            eng.wait_ge(h_ready, j * C2 + q - 1)
                        eng.activation(sg[:, q % 2].rearrange("p f s -> p (f s)"), ps[:, q % 2, 0:FPC * CAPW], ACT.Silu
                                       ).then_inc(silu_ready, 1)
                    eng.wait_ge(y_ready, j + 1)
                    eng.activation(Y, ps[:, 6:8, :].rearrange("p b n -> p (b n)"), ACT.Copy).then_inc(y_copied, 1)

            @block.vector
            def _(eng):
                chain(eng.memset(XT.rearrange("p k e s -> p (k e s)"), 0.0))
                eng.memset(facc.rearrange("p t d -> p (t d)"), 0.0).then_inc(acc_zero, 1)
                eng.wait_ge(acc_zero, 1)
                with eng.Fori(0, PAIRS) as j:
                    eng.tensor_tensor(selG, selL[:, :, bass.ds(j * 2, 2), :],
                                      aff[:, 1:TT, bass.ds(j * 2, 2)].unsqueeze(3).broadcast_to([P, 4, 2, CAP_L]),
                                      ALU.mult).then_inc(selg_done, 1)
                    eng.wait_ge(gather_ready, j + 1)
                    for k in range(KT):
                        bank, c0 = k // 3, (k % 3) * 2 * CAP
                        for v, b0, n, s0 in ((1, c0, CAP_L, 0), (0, c0 + 2 * CAP_L, CAP_C, CAP_L)):
                            src = ps[:, bank, b0:b0 + 2 * n].rearrange("p (e s) -> p e s", e=2)
                            eng.tensor_scalar(XT[:, k, :, s0:s0 + n], src, modT[:, 4, k, v:v + 1],
                                              modT[:, 3, k, v:v + 1], ALU.mult, ALU.add).then_inc(gather_done, 1)
                    for e in range(2):
                        for c in range(NC_F):
                            q = e * NC_F + c
                            eng.wait_ge(silu_ready, j * C2 + q + 1)
                            eng.tensor_tensor(H[:, e, c * FPC:(c + 1) * FPC, :], sg[:, q % 2],
                                              ps[:, q % 2, FPC * CAPW:2 * FPC * CAPW].rearrange("p (f s) -> p f s", f=FPC),
                                              ALU.mult).then_inc(h_ready, 1)
                        eng.wait_ge(chunk_used, j * PER_PAIR + ADA_CHUNKS + OUT_CHUNKS + (e + 1) * 3 * NC_F)
                        for b in range(2):
                            src = ps[:, 4 + b, 0:4 * CAPW].rearrange("p (k s) -> p k s", k=4)
                            g = modT[:, 5, 4 * b:4 * b + 4, :]
                            eng.tensor_tensor(YT[:, 4 * b:4 * b + 4, e * CAP_L:(e + 1) * CAP_L], src[:, :, 0:CAP_L],
                                              g[:, :, 1:2].broadcast_to([P, 4, CAP_L]), ALU.mult).then_inc(yt_done, 1)
                            eng.tensor_tensor(YcT[:, 4 * b:4 * b + 4, bass.ds(j * 2 * CAP_C + e * CAP_C, CAP_C)],
                                              src[:, :, CAP_L:CAP], g[:, :, 0:1].broadcast_to([P, 4, CAP_C]),
                                              ALU.mult).then_inc(yt_done, 1)
                    for s in range(8):
                        eng.wait_ge(scat_ready, j * 8 + s + 1 + PRIMED)
                        dst = facc[:, 1 + s // 2, (s % 2) * 512:(s % 2 + 1) * 512]
                        eng.tensor_tensor(dst, ps[:, 6 + s % 2, :], dst, ALU.add).then_inc(scat_added, 1)

        yc_ready = sem("yc_ready")
        yc_copied = sem("yc_copied")
        cscat_ready = sem("cscat_ready")
        cacc_done = sem("cacc_done")
        var2_ready = sem("var2_ready")
        std2_ready = sem("std2_ready")
        y_done = sem("y_done")
        stored = sem("stored")

        with nc.Block() as block:
            @block.sync
            def _(eng):
                for n, t in enumerate((1, 2, 3, 4, 0)):
                    eng.wait_ge(y_done, n + 1)
                    eng.dma_start(a["y"][t], x1[:, t, :]).then_inc(stored, 16)
                eng.wait_ge(stored, 16 * TT)

            @block.tensor
            def _(eng):
                for c in range(2):
                    if c:
                        eng.wait_ge(yc_copied, 1)
                    for k in range(KT):
                        mm = eng.transpose(ps[:, k // 4, (k % 4) * P:(k % 4 + 1) * P], YcT[:, k, c * P:(c + 1) * P], ident)
                    mm.then_inc(yc_ready, 1)
                    eng.wait_ge(yc_copied, c + 1)
                    for s in range(2):
                        mm = eng.matmul(ps[:, 2 + s, :], GTc[:, c, :], Y[:, s * 512:(s + 1) * 512],
                                        start=(c == 0), stop=(c == 1))
                    mm.then_inc(cscat_ready, 1)

            @block.scalar
            def _(eng):
                for c in range(2):
                    eng.wait_ge(yc_ready, c + 1)
                    if c:
                        eng.wait_ge(cscat_ready, 1)
                    eng.activation(Y, ps[:, 0:2, :].rearrange("p b n -> p (b n)"), ACT.Copy).then_inc(yc_copied, 1)
                for t in range(TT):
                    eng.wait_ge(var2_ready, t + 1)
                    eng.activation(bnag[:, 2:3], bnag[:, 1:2], ACT.Sqrt).then_inc(std2_ready, 1)

            @block.vector
            def _(eng):
                eng.wait_ge(route_landed, 16 * 6)
                for n, t in enumerate((1, 2, 3, 4, 0)):
                    x = x1[:, t, :]
                    if t == 0:
                        eng.wait_ge(cscat_ready, 2)
                        mix = ps[:, 2:4, :].rearrange("p b n -> p (b n)")
                    else:
                        mix = facc[:, t, :]
                    chain(eng.scalar_tensor_tensor(out=x, in0=x, scalar=ALPHA, in1=mix, op0=ALU.mult, op1=ALU.add))
                    layer_norm(eng, x, var2_ready, std2_ready, n)
                    chain(eng.tensor_tensor(x, x, lnG, ALU.mult))
                    eng.tensor_tensor(x, x, lnB, ALU.add).then_inc(y_done, 1)


def constants():
    j = np.arange(P)
    rot = np.zeros((P, P), np.float32)
    for m in range(P):
        if m % 32 < 16:
            rot[m + 16, m] = -1.0
        else:
            rot[m - 16, m] = 1.0
    t = np.arange(LAT)
    half = HD // 2
    inv = (np.float32(10000.0) ** (-np.arange(0, half, 2, dtype=np.float32) / np.float32(half))).astype(np.float32)
    ang_r = (t // GRID).astype(np.float32)[:, None] * inv[None, :]
    ang_c = (t % GRID).astype(np.float32)[:, None] * inv[None, :]
    ang = np.concatenate([ang_r, ang_r, ang_c, ang_c], axis=1).astype(np.float32)
    cos = np.concatenate([np.cos(ang).T, np.cos(ang).T], axis=0)
    sin = np.concatenate([np.sin(ang).T, np.sin(ang).T], axis=0)
    w = np.arange(GRID)
    c0 = np.clip(w - WIN_W // 2, 0, GRID - WIN_W)
    inside = (w[None, :] >= c0[:, None]) & (w[None, :] < c0[:, None] + WIN_W)
    mask = np.where(inside, 0.0, NEG).astype(np.float32)
    x = np.arange(P)
    hot = (x[None, :] == (GRID + WIN_W - 1) - np.arange(DC)[:, None]).astype(np.float32)
    return {
        "ident": np.eye(P, dtype=np.float32),
        "rotM": rot,
        "cosT": np.ascontiguousarray(cos, dtype=np.float32),
        "sinT": np.ascontiguousarray(sin, dtype=np.float32),
        "mask": np.concatenate([mask, mask], axis=0),
        "iota1": np.tile(np.arange(1, CAP_L + 1, dtype=np.float32), (P, 1)),
        "colhot": hot,
    }


def kernel(**inputs):
    import concourse.bacc as bacc
    from concourse.bass_utils import run_bass_kernel_spmd

    x = {k: np.asarray(v) for k, v in inputs.items()}

    def rows_to_chunks(w, cols):
        return w.reshape(KT, P, -1, cols).transpose(2, 1, 0, 3)

    tokens = np.concatenate([x["x_prompt"][0], x["x_sample"][0]], axis=0)
    w_in = x["w_in"][0].reshape(KT, P, 6, GROUPS, P)
    w_in = np.stack([w_in[:, :, [0, 1]], w_in[:, :, [3, 4]], w_in[:, :, [2, 5]]], axis=0)
    w_in = w_in.transpose(4, 0, 2, 1, 3, 5).reshape(GROUPS, 3, P, KT, 256)
    gate = x["w_gate"][0].reshape(E, KT, P, NC_F, 256).transpose(0, 3, 2, 1, 4).reshape(E, NC_F, 1, P, CW)
    up = x["w_up"][0].reshape(E, KT, P, NC_F, 256).transpose(0, 3, 2, 1, 4).reshape(E, NC_F, 1, P, CW)
    down = x["w_down"][0].reshape(E, NC_F, FPC, P, D).transpose(0, 1, 3, 2, 4).reshape(E, NC_F, P, CW)
    gu = np.concatenate([gate, up], axis=2).reshape(E, 2 * NC_F, P, CW)
    w_exp = np.concatenate([gu, down], axis=1).reshape(EXPERT_CHUNKS, P, CW)
    k_na = x["cache_na_k"][0, 0].reshape(GROUPS, 2, CTX, HD).transpose(0, 1, 3, 2).reshape(GROUPS, P, CTX)
    k_df = x["cache_diff_k"][0, 0].transpose(0, 1, 3, 2).reshape(GROUPS, P, CTX)
    v_na = x["cache_na_v"][0, 0].reshape(GROUPS, 2, CTX, HD).transpose(0, 2, 1, 3).reshape(GROUPS, CTX, P)
    v_df = x["cache_diff_v"][0, 0]
    arrays = constants()
    arrays.update({
        "x": tokens.reshape(TT, P, D),
        "xT": tokens.reshape(TOK, KT, P).transpose(2, 1, 0),
        "cvecs": np.stack([x["c_ctx"], x["c"][0]], axis=0).reshape(2, KT, P).transpose(2, 1, 0),
        "b_ada": x["b_ada"][0].reshape(6, KT, P).transpose(2, 0, 1),
        "w_ada": rows_to_chunks(x["w_ada"][0], 256).reshape(ADA_CHUNKS, P, CW),
        "w_out": rows_to_chunks(x["w_out"][0], 256).reshape(OUT_CHUNKS, P, CW),
        "w_in": w_in,
        "w_exp": w_exp,
        "w_router": x["w_router"][0].reshape(KT, P, E).transpose(1, 0, 2),
        "rpbT": x["na_rel_bias"][0].transpose(2, 0, 1),
        "lambdas": np.stack([x["lambda_q1"][0], x["lambda_k1"][0], x["lambda_q2"][0], x["lambda_k2"][0]], axis=0),
        "subln_g": x["subln_g"][0],
        "ln1_g": x["ln1_g"][0], "ln1_b": x["ln1_b"][0], "ln2_g": x["ln2_g"][0], "ln2_b": x["ln2_b"][0],
        "cacheKT": np.stack([k_na, k_df], axis=1),
        "cacheV": np.concatenate([v_na, v_df], axis=2),
    })
    nc = bacc.Bacc("TRN2", target_bir_lowering=False, num_devices=1)
    feed, aps = {}, {}
    for name, value in arrays.items():
        value = np.ascontiguousarray(value)
        feed[f"in_{name}"] = value
        aps[name] = nc.dram_tensor(f"in_{name}", value.shape, mybir.dt.from_np(value.dtype), kind="ExternalInput").ap()
    for name, shape in (("y", (TT, P, D)), ("k_new", (GROUPS, CTX, 256)), ("v_new", (GROUPS, CTX, 256))):
        aps[name] = nc.dram_tensor(f"out_{name}", shape, F32, kind="ExternalOutput").ap()
    build(nc, aps)
    r = run_bass_kernel_spmd(nc, [feed], core_ids=[0]).results[0]
    y, k_new, v_new = r["out_y"], r["out_k_new"], r["out_v_new"]
    y_prompt = y[0].reshape(1, CTX, D)
    y_sample = y[1:].reshape(1, LAT, D)
    na_k = k_new[:, :, :P].reshape(GROUPS, CTX, 2, HD).transpose(0, 2, 1, 3).reshape(1, 1, 2 * GROUPS, CTX, HD)
    na_v = v_new[:, :, :P].reshape(GROUPS, CTX, 2, HD).transpose(0, 2, 1, 3).reshape(1, 1, 2 * GROUPS, CTX, HD)
    df_k = k_new[:, :, P:].reshape(GROUPS, CTX, 2, HD).transpose(0, 2, 1, 3).reshape(1, 1, GROUPS, 2, CTX, HD)
    df_v = v_new[:, :, P:].reshape(1, 1, GROUPS, CTX, P)
    return (y_prompt, y_sample, na_k, na_v, df_k, df_v)
```

```python
import math
from contextlib import ExitStack

import numpy as np

import concourse.bass as bass
from concourse import mybir
from concourse.alu_op_type import AluOpType as ALU

F32 = mybir.dt.float32
F32R = mybir.dt.float32r
ACT = mybir.ActivationFunctionType
AX_X = mybir.AxisListType.X

P = 128
D = 1024
KT = D // P
CTX = 128
LAT = 512
TOK = CTX + LAT
TT = TOK // P
GRID = 64
ROWS = LAT // GRID
HD = 64
GROUPS = 4
WIN_H, WIN_W = 8, 16
DR = 2 * WIN_H - 1
DC = 2 * WIN_W - 1
BX = DR + 1
E = 16
CAP_L = 2 * LAT // E
CAP_C = 2 * CTX // E
CAP = CAP_L + CAP_C
STREAM = 96
SPLITS = 3
SPLIT_PRIMED = SPLITS
FF = 2816
FT = FF // P
CW = 2048
FPC = 2
NC_F = FT // FPC
RING = 6
ADA_CHUNKS = 24
OUT_CHUNKS = 4
FIRST_EXPERT_CHUNK = ADA_CHUNKS + OUT_CHUNKS
PER_PAIR = 2 * 3 * NC_F
EXPERT_CHUNKS = E * 3 * NC_F
PAIRS = E // 2
ALPHA = 2.0 ** 0.25
EPS = 1e-5
LAMBDA_INIT = 0.8 - 0.6 * math.exp(-0.3 * 0)
SCALE = HD ** -0.5
NEG = -1e30
PRIMED = 1


class Tally:

    def __init__(self, sem):
        self.sem, self.base, self.i, self.per, self.k = sem, 0, None, 0, 0

    def enter(self, i, per):
        self.base, self.i, self.per, self.k = self.base + self.k, i, per, 0

    def leave(self, iterations):
        assert self.k == self.per, (self.k, self.per)
        self.base, self.i, self.k = self.base + self.per * iterations, None, 0

    def value(self):
        return self.base + self.k if self.i is None else self.i * self.per + (self.base + self.k)


def units():
    out, s = [], 0
    for h in range(2):
        for t in range(TT):
            out.append(("na", h, t, 640 if t else CTX, [s]))
            s += 1
    for t in range(TT):
        out.append(("df", 0, t, 640 if t else CTX, [s, s + 1]))
        s += 2
    return out, s


def build(nc, a):
    ctx = ExitStack()
    with ctx:
        def sem(name):
            return ctx.enter_context(nc.semaphore(name))

        ring = ctx.enter_context(nc.sbuf_tensor("ring", [P, RING, CW], F32))
        ps = ctx.enter_context(nc.psum_tensor("ps", [P, 8, 512], F32))
        bias_scratch = nc.dram_tensor("bias_scratch", [GROUPS, P, 2 * BX * GRID], F32, kind="Internal").ap()
        gate_scratch = nc.dram_tensor("gate_scratch", [2, 2, KT, P], F32, kind="Internal").ap()

        places = [ctx]
        count = [0]

        def take(n, dtype=F32):
            count[0] += 1
            return places[-1].enter_context(nc.sbuf_tensor(f"place{count[0]}", [P, n], dtype))[:, :]

        ident = take(P)
        modT = take(6 * KT * 2).rearrange("p (m k v) -> p m k v", m=6, k=KT)
        wroute = take(KT * E).rearrange("p (k e) -> p k e", k=KT)
        iota1 = take(CAP_L)
        subg = take(P)
        lam_s = take(8)
        cosT = take(LAT)
        sinT = take(LAT)
        rotM = take(P)
        silu_c = take(2 * KT).rearrange("p (k v) -> p k v", k=KT)
        badaT = take(6 * KT).rearrange("p (m k) -> p m k", m=6)
        stat = take(20 * 4).rearrange("p (s c) -> p s c", c=4)
        rec = take(15 * 2).rearrange("p (s c) -> p s c", c=2)
        bnst = take(12).rearrange("p (a c) -> p a c", a=2)
        bnag = take(4)
        rms = take(3 * 20).rearrange("p (c n) -> p c n", c=3)
        xT = take(KT * TOK).rearrange("p (k t) -> p k t", k=KT)
        x1 = xT.rearrange("p k t -> p (k t)").rearrange("p (t d) -> p t d", t=TT)
        O = take(TT * D).rearrange("p (t d) -> p t d", t=TT)
        facc = O
        def weights(slot):
            return ring[:, slot, :].rearrange("p (k n) -> p k n", k=KT)

        const_landed = sem("const_landed")
        tokens_landed = sem("tokens_landed")
        landed = [sem(f"chunk_landed{i}") for i in range(RING)]
        chunk_used = sem("chunk_used")
        dve_own = Tally(sem("dve_own"))

        def chunk_source(n):
            if n < ADA_CHUNKS:
                return a["w_ada"][n]
            return a["w_out"][n - ADA_CHUNKS]

        def issue(eng, n):
            if n >= RING:
                eng.wait_ge(chunk_used, n - RING + 1)
            src = chunk_source(n) if n < FIRST_EXPERT_CHUNK else a["w_exp"][n - FIRST_EXPERT_CHUNK]
            eng.dma_start(ring[:, n % RING, :], src).then_inc(landed[n % RING], 16)

        def arrived(eng, n):
            eng.wait_ge(landed[n % RING], 16 * (n // RING + 1))

        def chain(ins):
            ins.then_inc(dve_own.sem, 1)
            dve_own.k += 1
            nc.vector.wait_ge(dve_own.sem, dve_own.value())

        def layer_norm(eng, x, var_sem, std_sem, t):
            for c in range(2):
                chain(eng.bn_stats(bnst[:, c, :], x[:, c * 512:(c + 1) * 512]))
            chain(eng.bn_aggr(bnag[:, 0:2], bnst))
            eng.tensor_scalar(bnag[:, 1:2], bnag[:, 1:2], EPS, None, ALU.add).then_inc(var_sem, 1)
            eng.wait_ge(std_sem, t + 1)
            chain(eng.reciprocal(bnag[:, 3:4], bnag[:, 2:3]))
            chain(eng.tensor_scalar(x, x, bnag[:, 0:1], bnag[:, 3:4], ALU.subtract, ALU.mult))

        v_ready = sem("v_ready")
        negmax_ready = sem("negmax_ready")
        o_ready = sem("o_ready")
        p_ready = sem("p_ready")
        pt_copied = sem("pt_copied")
        o_done = sem("o_done")
        k_stored = sem("k_stored")
        v_stored = sem("v_stored")
        scat_ready = sem("scat_ready")
        scat_added = sem("scat_added")

        places.append(ctx.enter_context(ExitStack()))
        tables = take(2 * GROUPS * BX * GRID).rearrange("p (h x c) -> p h x c", h=2 * GROUPS, x=BX)
        mask = take(GRID)
        colhot = take(P)
        rpbT = take(P)
        lam_in = take(4 * HD).rearrange("p (m d) -> p m d", m=4)
        lam_tmp = take(HD)
        silu_w = take(KT * STREAM).rearrange("p (k v) -> p k v", k=KT)


        silu_done = sem("silu_done")
        mod_done = sem("mod_done")
        tab_ready = sem("tab_ready")
        tab_copied = sem("tab_copied")
        tab_stored = sem("tab_stored")
        ada_added = sem("ada_added")
        wide_zero = sem("wide_zero")
        rpb_zero = sem("rpb_zero")
        gates_stored = sem("gates_stored")
        h_done = sem("h_done")
        CK = 4
        HR = P
        CONSTS = [(ident, "ident"), (rotM, "rotM"), (cosT, "cosT"), (sinT, "sinT"), (mask, "mask"),
                  (iota1, "iota1"), (silu_c, "cvecs"), (badaT, "b_ada"), (wroute, "w_router")]
        n_const = len(CONSTS) + 4

        with nc.Block() as block:
            @block.sync
            def _(eng):
                for primed in (v_ready, negmax_ready, o_ready, p_ready, pt_copied, o_done, k_stored, v_stored,
                               scat_ready, scat_added):
                    eng.sem_inc(primed, PRIMED)
                for dst, name in CONSTS:
                    eng.dma_start(dst, a[name]).then_inc(const_landed, 16)
                eng.dma_start(colhot[0:DC], a["colhot"]).then_inc(const_landed, 16)
                eng.wait_ge(rpb_zero, 1)
                eng.dma_start(rpbT[0:DC, 0:2 * GROUPS * DR], a["rpbT"].rearrange("c h r -> c (h r)")).then_inc(const_landed, 16)
                eng.dma_start(lam_in, a["lambdas"].partition_broadcast(P)).then_inc(const_landed, 16)
                eng.dma_start(subg, a["subln_g"].partition_broadcast(P)).then_inc(const_landed, 16)
                for n in range(RING):
                    issue(eng, n)
                eng.dma_start(xT, a["xT"]).then_inc(tokens_landed, 16)
                for n in range(RING, ADA_CHUNKS + RING):
                    issue(eng, n)

            @block.gpsimd
            def _(eng):
                eng.memset(rpbT, 0.0).then_inc(rpb_zero, 1)
                eng.wait_ge(tab_copied, 2 * GRID // CK)
                for g in range(GROUPS):
                    eng.dma_start(bias_scratch[g], tables[:, 2 * g:2 * g + 2].rearrange("p h x c -> p (h x c)")
                                  ).then_inc(tab_stored, 16)
                eng.wait_ge(tab_stored, 16 * GROUPS)

            @block.scalar
            def _(eng):
                eng.wait_ge(const_landed, 16 * n_const)
                eng.wait_ge(wide_zero, 1)
                eng.activation(silu_w[:, :, 0:2], silu_c, ACT.Silu).then_inc(silu_done, 1)
                eng.wait_ge(mod_done, 1)
                eng.wait_ge(tokens_landed, 16)
                for k in range(0, KT, 2):
                    for v, t0, t1 in ((0, 0, CTX), (1, CTX, TOK)):
                        eng.activation(xT[:, k, t0:t1], xT[:, k, t0:t1], ACT.Identity,
                                       bias=modT[:, 0, k, v:v + 1], scale=modT[:, 1, k, v:v + 1]
                                       ).then_inc(h_done, 1)

            @block.tensor
            def _(eng):
                eng.wait_ge(const_landed, 16 * n_const)
                for b in range(GRID // CK):
                    if b >= 4:
                        eng.wait_ge(tab_copied, 2 * (b - 3))
                    for c in range(CK):
                        s = GRID - (b * CK + c)
                        for half in range(2):
                            mm = eng.matmul(ps[64 * half:64 * half + 64, b % 4, c * HR:(c + 1) * HR],
                                            colhot[0:DC, s:s + GRID], rpbT[0:DC, :], start=True, stop=True)
                    mm.then_inc(tab_ready, 1)
                eng.wait_ge(silu_done, 1)
                for n in range(ADA_CHUNKS):
                    arrived(eng, n)
                    if n >= 4:
                        eng.wait_ge(ada_added, n - 3)
                    w = weights(n % RING)
                    for j in range(2):
                        for k in range(KT):
                            mm = eng.matmul(ps[:, 4 + n % 4, j * STREAM:(j + 1) * STREAM], w[:, k, j * P:(j + 1) * P],
                                            silu_w[:, k, :], start=(k == 0), stop=(k == KT - 1))
                    mm.then_inc(chunk_used, 1)

            @block.vector
            def _(eng):
                eng.wait_ge(const_landed, 16 * n_const)
                eng.memset(silu_w.rearrange("p k v -> p (k v)"), 0.0).then_inc(wide_zero, 1)
                chain(eng.memset(tables.rearrange("p h x c -> p (h x c)"), 0.0))
                for b in range(GRID // CK):
                    eng.wait_ge(tab_ready, b + 1)
                    for half in range(2):
                        p0 = 64 * half
                        src = ps[p0:p0 + 64, b % 4, :].rearrange("p (c n) -> p c n", c=CK)[:, :, 0:2 * GROUPS * DR]
                        dst = tables[p0:p0 + 64, :, half:half + DR, b * CK:(b + 1) * CK]
                        m = mask[p0:p0 + 64, b * CK:(b + 1) * CK].unsqueeze(1).unsqueeze(1)
                        eng.tensor_tensor(dst, src.rearrange("p c (h r) -> p h r c", r=DR),
                                          m.broadcast_to([64, 2 * GROUPS, DR, CK]), ALU.add).then_inc(tab_copied, 1)
                for m in range(2):
                    chain(eng.tensor_tensor_reduce(lam_tmp, lam_in[:, 2 * m, :], lam_in[:, 2 * m + 1, :], 1.0, 0.0,
                                                   ALU.mult, ALU.add, lam_s[:, m:m + 1]))
                flat, b_flat = modT.rearrange("p m k v -> p (m k) v"), badaT.rearrange("p m k -> p (m k)")
                for n in range(ADA_CHUNKS):
                    eng.wait_ge(chunk_used, n + 1)
                    src = ps[:, 4 + n % 4, 0:2 * STREAM].rearrange("p (j c) -> p j c", j=2)[:, :, 0:2]
                    eng.tensor_tensor(flat[:, 2 * n:2 * n + 2, :], src,
                                      b_flat[:, 2 * n:2 * n + 2].unsqueeze(2).broadcast_to([P, 2, 2]), ALU.add
                                      ).then_inc(ada_added, 1)
                eng.wait_ge(ada_added, ADA_CHUNKS)
                for m in (1, 4):
                    ins = eng.tensor_scalar(modT[:, m], modT[:, m], 1.0, None, ALU.add)
                    if m == 1:
                        chain(ins)
                ins.then_inc(mod_done, 1)
                eng.wait_ge(mod_done, 1)
                eng.wait_ge(tokens_landed, 16)
                for k in range(1, KT, 2):
                    for v, t0, t1 in ((0, 0, CTX), (1, CTX, TOK)):
                        eng.tensor_scalar(xT[:, k, t0:t1], xT[:, k, t0:t1], modT[:, 1, k, v:v + 1],
                                          modT[:, 0, k, v:v + 1], ALU.mult, ALU.add).then_inc(h_done, 1)

        places.pop().close()
        places.append(ctx.enter_context(ExitStack()))
        win = take(3 * CW).rearrange("p (s k n) -> p s k n", s=3, k=KT)
        bias = take(2 * BX * GRID).rearrange("p (h x c) -> p h x c", h=2, x=BX)
        qna = [take(TOK) for _ in range(2)]
        kna = take(TOK + CTX)
        qdfm = [take(TOK) for _ in range(2)]
        kdf = take(TOK + CTX)
        V = take((TT + 1) * 256).rearrange("p (t n) -> p t n", t=TT + 1)
        Pb = take(4 * 640).rearrange("p (b n) -> p b n", b=4)
        PT = take(2 * 640).rearrange("p (b n) -> p b n", b=2)
        qdf = PT[:, 0, :]
        kout = take(256)

        U, S_STEPS = units()
        NU = len(U)
        win_landed = [sem(f"win_landed{i}") for i in range(3)]
        bias_landed = sem("bias_landed")
        cache_landed = sem("cache_landed")
        qk_ready = sem("qk_ready")
        qk_copied = sem("qk_copied")
        v_copied = sem("v_copied")
        rot_ready = sem("rot_ready")
        rope_done = sem("rope_done")
        kctx_ready = sem("kctx_ready")
        kctx_copied = sem("kctx_copied")
        s_ready = sem("s_ready")
        a_ready = sem("a_ready")
        pt_ready = sem("pt_ready")
        lam_exp = sem("lam_exp")
        q_zero = sem("q_zero")

        with nc.Block() as block:
            @block.sync
            def _(eng):
                with eng.Fori(0, GROUPS) as i:
                    eng.wait_ge(v_ready, i * TT + PRIMED)
                    for s in range(3):
                        eng.dma_start(win[:, s], a["w_in"][i, s]).then_inc(win_landed[s], 16)
                    eng.wait_ge(negmax_ready, i * S_STEPS + PRIMED)
                    eng.dma_start(bias.rearrange("p h x c -> p (h x c)"), bias_scratch[i]).then_inc(bias_landed, 16)
                    eng.wait_ge(o_ready, i * NU + PRIMED)
                    eng.dma_start(kna[:, TOK:], a["cacheKT"][i, 0]).then_inc(cache_landed, 16)
                    eng.dma_start(kdf[:, TOK:], a["cacheKT"][i, 1]).then_inc(cache_landed, 16)
                    eng.dma_start(V[:, TT, :], a["cacheV"][i]).then_inc(cache_landed, 16)
                    eng.wait_ge(v_copied, i * TT + 1)
                    eng.dma_start(a["v_new"][i], V[:, 0, :]).then_inc(v_stored, 16)
                    eng.wait_ge(kctx_copied, i + 1)
                    eng.dma_start(a["k_new"][i], kout).then_inc(k_stored, 16)
                eng.wait_ge(v_stored, 16 * GROUPS + PRIMED)
                eng.wait_ge(k_stored, 16 * GROUPS + PRIMED)

            @block.gpsimd
            def _(eng):
                with nc.allow_non_contiguous_dma(reason="8 KiB turned from columns into rows"):
                    for n, m in enumerate((2, 5)):
                        for v in range(2):
                            for k in range(KT):
                                eng.dma_start(gate_scratch[n, v, k].unsqueeze(1), modT[:, m, k, v:v + 1]
                                              ).then_inc(gates_stored, 16)
                eng.wait_ge(gates_stored, 16 * 4 * KT)

            @block.tensor
            def _(eng):
                eng.wait_ge(h_done, 2 * KT)
                with eng.Fori(0, GROUPS) as i:
                    eng.wait_ge(p_ready, i * S_STEPS + PRIMED)
                    eng.wait_ge(pt_copied, i * NU + PRIMED)
                    eng.wait_ge(o_done, i * NU + PRIMED)
                    for g in range(4):
                        if g % 2 == 0:
                            eng.wait_ge(win_landed[g // 2], i * 16 + 16)
                        w = win[:, g // 2]
                        for bank, t0, t1 in ((2 * g, CTX, TOK), (2 * g + 1, 0, CTX)):
                            for k in range(KT):
                                mm = eng.matmul(ps[:, bank, 0:t1 - t0], w[:, k, (g % 2) * P:(g % 2 + 1) * P],
                                                xT[:, k, t0:t1], start=(k == 0), stop=(k == KT - 1))
                        mm.then_inc(qk_ready, 1)
                    eng.wait_ge(win_landed[2], i * 16 + 16)
                    for t in range(TT):
                        if t == 3:
                            eng.wait_ge(qk_copied, i * 4 + 4)
                            for n, src in enumerate((qdf, kdf)):
                                eng.matmul(ps[:, 5 + n, :], rotM, src[:, CTX:TOK], start=True, stop=True
                                           ).then_inc(rot_ready, 1)
                            for n, src in enumerate((kna, kdf)):
                                mm = eng.transpose(ps[:, 7, n * P:(n + 1) * P], src[:, 0:CTX], ident)
                            mm.then_inc(kctx_ready, 1)
                        eng.wait_ge(qk_copied, i * 4 + t // 2 + 1)
                        for k in range(KT):
                            mm = eng.matmul(ps[:, t, 0:256], xT[:, k, t * P:(t + 1) * P], win[:, 2, k, :],
                                            start=(k == 0), stop=(k == KT - 1))
                        mm.then_inc(v_ready, 1)
                    eng.wait_ge(v_copied, i * TT + TT)
                    eng.wait_ge(kctx_copied, i + 1)
                    eng.wait_ge(rope_done, i * 2 + 2)
                    eng.wait_ge(cache_landed, i * 48 + 48)

                    def scores(u):
                        kind, h, t, n, steps = U[u]
                        for m, s in enumerate(steps):
                            q, kk = (qna[h], kna) if kind == "na" else (qdfm[m], kdf)
                            if s >= 2:
                                eng.wait_ge(p_ready, i * S_STEPS + (s - 1) + PRIMED)
                            b = 2 * (s % 2)
                            lhs = q[:, t * P:(t + 1) * P]
                            if t == 0:
                                mm = eng.matmul(ps[:, b, 0:CTX], lhs, kk[:, 0:CTX], start=True, stop=True)
                            else:
                                eng.matmul(ps[:, b, 0:LAT], lhs, kk[:, CTX:TOK], start=True, stop=True)
                                mm = eng.matmul(ps[:, b + 1, 0:CTX], lhs, kk[:, TOK:], start=True, stop=True)
                            mm.then_inc(s_ready, 1)

                    def turn(u):
                        kind, h, t, n, steps = U[u]
                        if kind == "na":
                            eng.wait_ge(p_ready, i * S_STEPS + steps[0] + 1 + PRIMED)
                        else:
                            eng.wait_ge(a_ready, i * TT + t + 1)
                        if u >= 1:
                            eng.wait_ge(pt_copied, i * NU + u + PRIMED)
                        for c in range(n // P):
                            mm = eng.transpose(ps[:, 4 + c // 4, (c % 4) * P:(c % 4 + 1) * P],
                                               Pb[:, steps[0] % 4, c * P:(c + 1) * P], ident)
                        mm.then_inc(pt_ready, 1)

                    def weigh(u):
                        kind, h, t, n, steps = U[u]
                        eng.wait_ge(pt_copied, i * NU + u + 1 + PRIMED)
                        if u >= 2:
                            eng.wait_ge(o_done, i * NU + u - 1 + PRIMED)
                        c0, c1 = (0, P) if kind == "na" else (P, 2 * P)
                        for c in range(n // P):
                            mm = eng.matmul(ps[:, 6 + u % 2, 0:c1 - c0], PT[:, u % 2, c * P:(c + 1) * P],
                                            V[:, c + 1 if t else 0, c0:c1], start=(c == 0), stop=(c == n // P - 1))
                        mm.then_inc(o_ready, 1)

                    for k in range(NU + 2):
                        if k < NU:
                            scores(k)
                        if k >= 2:
                            weigh(k - 2)
                        if 1 <= k <= NU:
                            turn(k - 1)

            @block.scalar
            def _(eng):
                eng.wait_ge(q_zero, 4)
                for m in range(2):
                    ins = eng.activation(lam_s[:, 2 + m:3 + m], lam_s[:, m:m + 1], ACT.Exp)
                ins.then_inc(lam_exp, 1)
                with eng.Fori(0, GROUPS) as i:
                    for g, dst in enumerate((None, kna, qdf, kdf)):
                        eng.wait_ge(qk_ready, i * 4 + g + 1)
                        sc = SCALE if g % 2 == 0 else 1.0
                        parts = [(0, P, dst)] if g else [(0, 64, qna[0]), (64, P, qna[1])]
                        for p0, p1, x in parts:
                            eng.activation(x[p0:p1, CTX:TOK], ps[p0:p1, 2 * g, :], ACT.Copy, scale=sc)
                            ins = eng.activation(x[p0:p1, 0:CTX], ps[p0:p1, 2 * g + 1, 0:CTX], ACT.Copy, scale=sc)
                        ins.then_inc(qk_copied, 1)
                    eng.wait_ge(kctx_ready, i + 1)
                    eng.wait_ge(k_stored, i * 16 + PRIMED)
                    eng.activation(kout, ps[:, 7, 0:256], ACT.Copy).then_inc(kctx_copied, 1)

                    def exps(u):
                        kind, h, t, n, steps = U[u]
                        for s in steps:
                            eng.wait_ge(negmax_ready, i * S_STEPS + s + 1 + PRIMED)
                            if s >= 4:
                                user = [w for w in range(NU) if s - 4 in U[w][4]][0]
                                eng.wait_ge(pt_ready, i * NU + user + 1)
                            b = 2 * (s % 2)
                            src = ps[:, b:b + 2, :].rearrange("p b n -> p (b n)")[:, 0:n]
                            eng.activation(Pb[:, s % 4, 0:n], src, ACT.Exp, bias=stat[:, s, 2:3], scale=1.0,
                                           accum_out=stat[:, s, 3:4]).then_inc(p_ready, 1)

                    def copy_turned(u):
                        kind, h, t, n, steps = U[u]
                        eng.wait_ge(pt_ready, i * NU + u + 1)
                        eng.wait_ge(o_ready, i * NU + max(u - 1, 0) + PRIMED)
                        src = ps[:, 4:6, :].rearrange("p b n -> p (b n)")[:, 0:n]
                        eng.activation(PT[:, u % 2, 0:n], src, ACT.Copy).then_inc(pt_copied, 1)

                    for k in range(NU + 1):
                        if k < NU:
                            exps(k)
                        if k >= 1:
                            copy_turned(k - 1)

            @block.vector
            def _(eng):
                for x in (*qna, *qdfm):
                    eng.memset(x, 0.0).then_inc(q_zero, 1)
                eng.wait_ge(lam_exp, 1)
                chain(eng.tensor_tensor(lam_s[:, 4:5], lam_s[:, 3:4], lam_s[:, 2:3], ALU.subtract))
                chain(eng.tensor_scalar(lam_s[:, 4:5], lam_s[:, 4:5], -LAMBDA_INIT, None, ALU.add))
                with eng.Fori(0, GROUPS) as i:
                    dve_own.enter(i, 4 + 2 * (TT - 1) + 2 * TT + 3 * TT)
                    def copy_values(t):
                        eng.wait_ge(v_ready, i * TT + t + 1 + PRIMED)
                        eng.tensor_copy(V[:, t, :], ps[:, t, 0:256]).then_inc(v_copied, 1)

                    eng.wait_ge(v_stored, i * 16 + PRIMED)
                    for t in range(3):
                        copy_values(t)
                    for n, x in enumerate((qdf, kdf)):
                        eng.wait_ge(rot_ready, i * 2 + n + 1)
                        lat = x[:, CTX:TOK]
                        tmp = Pb[:, n, 0:LAT]
                        eng.wait_ge(qk_copied, i * 4 + 3 + n)
                        chain(eng.tensor_tensor(tmp, ps[:, 5 + n, :], sinT, ALU.mult))
                        chain(eng.tensor_tensor(lat, lat, cosT, ALU.mult))
                        if n == 0:
                            for p0, x2 in ((0, qdfm[0]), (64, qdfm[1])):
                                eng.tensor_copy(x2[p0:p0 + 64, 0:CTX], x[p0:p0 + 64, 0:CTX])
                                ins = eng.tensor_tensor(x2[p0:p0 + 64, CTX:TOK], lat[p0:p0 + 64], tmp[p0:p0 + 64], ALU.add)
                            ins.then_inc(rope_done, 1)
                        else:
                            eng.tensor_tensor(lat, lat, tmp, ALU.add).then_inc(rope_done, 1)

                    for t in range(3, TT):
                        copy_values(t)

                    def maxima(u):
                        kind, h, t, n, steps = U[u]
                        for s in steps:
                            eng.wait_ge(s_ready, i * S_STEPS + s + 1)
                            b = 2 * (s % 2)
                            src = ps[:, b:b + 2, :].rearrange("p b n -> p (b n)")
                            if kind == "na" and t:
                                if s == 1:
                                    eng.wait_ge(bias_landed, i * 16 + 16)
                                x0 = DR - ROWS - 2 * (t - 1)
                                table = bias[:, h, x0:x0 + ROWS, :].rearrange("p x c -> p (x c)")
                                eng.tensor_reduce(stat[:, s, 1:2], src[:, LAT:n], AX_X, ALU.max)
                                chain(eng.tensor_tensor_reduce(src[:, 0:LAT], src[:, 0:LAT], table, 1.0, -3e38, ALU.add,
                                                               ALU.max, stat[:, s, 0:1]))
                                eng.tensor_reduce(stat[:, s, 2:3], stat[:, s, 0:2], AX_X, ALU.max,
                                                  negate=True).then_inc(negmax_ready, 1)
                            else:
                                eng.tensor_reduce(stat[:, s, 2:3], src[:, 0:n], AX_X, ALU.max,
                                                  negate=True).then_inc(negmax_ready, 1)

                    def combine(u):
                        kind, h, t, n, steps = U[u]
                        s0, s1 = steps[0], steps[-1]
                        eng.wait_ge(p_ready, i * S_STEPS + s1 + 1 + PRIMED)
                        chain(eng.reciprocal(rec[:, u, 0:1], stat[:, s0, 3:4]))
                        if kind == "df":
                            chain(eng.reciprocal(rec[:, u, 1:2], stat[:, s1, 3:4]))
                            chain(eng.tensor_scalar(rec[:, u, 1:2], rec[:, u, 1:2], stat[:, s0, 3:4], lam_s[:, 4:5],
                                                    ALU.mult, ALU.mult))
                            eng.scalar_tensor_tensor(out=Pb[:, s0 % 4, 0:n], in0=Pb[:, s1 % 4, 0:n],
                                                     scalar=rec[:, u, 1:2], in1=Pb[:, s0 % 4, 0:n],
                                                     op0=ALU.mult, op1=ALU.add).then_inc(a_ready, 1)

                    def outputs(u):
                        kind, h, t, n, steps = U[u]
                        eng.wait_ge(o_ready, i * NU + u + 1 + PRIMED)
                        w = HD if kind == "na" else 2 * HD
                        off = 64 * h if kind == "na" else LAT
                        eng.tensor_scalar(O[:, t, bass.ds(i * P + off, w)], ps[:, 6 + u % 2, h * HD:h * HD + w], rec[:, u, 0:1],
                                          None, ALU.mult).then_inc(o_done, 1)

                    for k in range(NU + 2):
                        if 1 <= k <= NU:
                            combine(k - 1)
                        if k < NU:
                            maxima(k)
                        if k >= 2:
                            outputs(k - 2)
                dve_own.leave(GROUPS)

        places.pop().close()
        selL = take(4 * E * CAP_L).rearrange("p (t e s) -> p t e s", t=4, e=E)
        selC = take(E * CAP_C).rearrange("p (e s) -> p e s", e=E)
        aff = take(TT * E).rearrange("p (t e) -> p t e", t=TT)
        lnG = take(D)
        lnB = take(D)
        places.append(ctx.enter_context(ExitStack()))
        G1 = take(2 * D).rearrange("p (v d) -> p v d", v=2)
        OT = take(D).rearrange("p (k t) -> p k t", k=KT)
        h2T = take(D).rearrange("p (k t) -> p k t", k=KT)
        amax = take(TT)
        asum = take(TT)
        affT = take(TOK)
        work = take(TOK)
        picked = take(TOK)
        rank = take(TOK)
        zeros = take(TOK)
        top8 = take(8)
        pos = take(TT * E).rearrange("p (t e) -> p t e", t=TT)
        scr = take(D)

        route_landed = sem("route_landed")
        rms_sq = sem("rms_sq")
        rms_rt = sem("rms_rt")
        o_scaled = sem("o_scaled")
        ot_ready = sem("ot_ready")
        ot_copied = sem("ot_copied")
        proj_ready = sem("proj_ready")
        proj_done = sem("proj_done")
        var_ready = sem("var_ready")
        std_ready = sem("std_ready")
        x1_done = sem("x1_done")
        xt_ready = sem("xt_ready")
        h2_done = sem("h2_done")
        logit_ready = sem("logit_ready")
        logit_sub = sem("logit_sub")
        aff_exp = sem("aff_exp")
        aff_done = sem("aff_done")
        afft_ready = sem("afft_ready")
        rank_done = sem("rank_done")
        pos_ready = sem("pos_ready")
        sel_done = sem("sel_done")
        NT = TT * GROUPS

        with nc.Block() as block:
            @block.sync
            def _(eng):
                eng.dma_start(x1, a["x"].rearrange("t p d -> p t d")).then_inc(route_landed, 16)
                eng.dma_start(G1, gate_scratch[0].rearrange("v k p -> v (k p)").partition_broadcast(P)).then_inc(route_landed, 16)
                eng.dma_start(lnG, a["ln1_g"].partition_broadcast(P)).then_inc(route_landed, 16)
                eng.dma_start(lnB, a["ln1_b"].partition_broadcast(P)).then_inc(route_landed, 16)
                for n in range(ADA_CHUNKS + RING, ADA_CHUNKS + RING + OUT_CHUNKS):
                    issue(eng, n)
                eng.wait_ge(x1_done, TT)
                eng.dma_start(lnG, a["ln2_g"].partition_broadcast(P)).then_inc(route_landed, 16)
                eng.dma_start(lnB, a["ln2_b"].partition_broadcast(P)).then_inc(route_landed, 16)

            @block.tensor
            def _(eng):
                for t in range(TT):
                    eng.wait_ge(o_scaled, t + 1)
                    if t >= 1:
                        eng.wait_ge(ot_copied, t)
                    for k in range(KT):
                        mm = eng.transpose(ps[:, k // 4, (k % 4) * P:(k % 4 + 1) * P], O[:, t, k * P:(k + 1) * P], ident)
                    mm.then_inc(ot_ready, 1)
                    eng.wait_ge(ot_copied, t + 1)
                    if t >= 1:
                        eng.wait_ge(proj_done, t)
                    for c in range(OUT_CHUNKS):
                        n = ADA_CHUNKS + c
                        if t == 0:
                            arrived(eng, n)
                        for k in range(KT):
                            mm = eng.matmul(ps[:, 2 + c // 2, (c % 2) * 256:(c % 2 + 1) * 256], OT[:, k, :],
                                            weights(n % RING)[:, k, :], start=(k == 0), stop=(k == KT - 1))
                        if t == TT - 1:
                            mm.then_inc(chunk_used, 1)
                    if t < TT - 1:
                        mm.then_inc(proj_ready, 1)
                for t in range(TT):
                    eng.wait_ge(x1_done, t + 1)
                    if t >= 1:
                        eng.wait_ge(h2_done, t)
                    for k in range(KT):
                        mm = eng.transpose(ps[:, 4 + k // 4, (k % 4) * P:(k % 4 + 1) * P], x1[:, t, k * P:(k + 1) * P], ident)
                    mm.then_inc(xt_ready, 1)
                    eng.wait_ge(h2_done, t + 1)
                    for k in range(KT):
                        mm = eng.matmul(ps[:, 7, t * E:(t + 1) * E], h2T[:, k, :], wroute[:, k, :],
                                        start=(k == 0), stop=(k == KT - 1))
                    mm.then_inc(logit_ready, 1)
                eng.wait_ge(aff_done, 1)
                for t in range(TT):
                    mm = eng.transpose(ps[0:E, t // 4, (t % 4) * P:(t % 4 + 1) * P], aff[:, t, :], ident)
                mm.then_inc(afft_ready, 1)
                eng.wait_ge(rank_done, 1)
                for t in range(TT):
                    mm = eng.transpose(ps[:, 2, t * E:(t + 1) * E], rank[0:E, t * P:(t + 1) * P], ident[0:E, 0:E])
                mm.then_inc(pos_ready, 1)

            @block.scalar
            def _(eng):
                eng.wait_ge(rms_sq, 1)
                eng.activation(rms[:, 1, :], rms[:, 0, :], ACT.Sqrt).then_inc(rms_rt, 1)
                for t in range(TT):
                    eng.wait_ge(ot_ready, t + 1)
                    if t >= 1:
                        eng.wait_ge(proj_ready, t)
                    eng.activation(OT.rearrange("p k t -> p (k t)"), ps[:, 0:2, :].rearrange("p b n -> p (b n)"),
                                   ACT.Copy).then_inc(ot_copied, 1)
                    eng.wait_ge(var_ready, t + 1)
                    eng.activation(bnag[:, 2:3], bnag[:, 1:2], ACT.Sqrt).then_inc(std_ready, 1)
                for t in range(TT):
                    eng.wait_ge(xt_ready, t + 1)
                    if t >= 1:
                        eng.wait_ge(logit_ready, t)
                    v = min(t, 1)
                    for k in range(KT):
                        ins = eng.activation(h2T[:, k, :], ps[:, 4 + k // 4, (k % 4) * P:(k % 4 + 1) * P], ACT.Identity,
                                             bias=modT[:, 3, k, v:v + 1], scale=modT[:, 4, k, v:v + 1])
                    ins.then_inc(h2_done, 1)
                eng.wait_ge(logit_sub, 1)
                eng.activation(aff, aff, ACT.Exp).then_inc(aff_exp, 1)

            @block.vector
            def _(eng):
                n = 0
                for t in range(TT):
                    for h in range(GROUPS):
                        part = O[:, t, LAT + h * P:LAT + (h + 1) * P]
                        ins = eng.tensor_tensor_reduce(scr[:, 0:P], part, part, 1.0 / P, EPS, ALU.mult, ALU.add,
                                                       rms[:, 0, n:n + 1])
                        n += 1
                        if n < TT * GROUPS:
                            chain(ins)
                ins.then_inc(rms_sq, 1)
                eng.wait_ge(rms_rt, 1)
                chain(eng.reciprocal(rms[:, 2, :], rms[:, 1, :]))
                chain(eng.tensor_scalar(subg, subg, 1.0 - LAMBDA_INIT, None, ALU.mult))
                n = 0
                for t in range(TT):
                    for h in range(GROUPS):
                        part = O[:, t, LAT + h * P:LAT + (h + 1) * P]
                        ins = eng.scalar_tensor_tensor(out=part, in0=part, scalar=rms[:, 2, n:n + 1], in1=subg,
                                                       op0=ALU.mult, op1=ALU.mult)
                        n += 1
                    ins.then_inc(o_scaled, 1)
                eng.wait_ge(route_landed, 16 * 4)
                for t in range(TT):
                    v = min(t, 1)
                    if t < TT - 1:
                        eng.wait_ge(proj_ready, t + 1)
                    else:
                        eng.wait_ge(chunk_used, ADA_CHUNKS + OUT_CHUNKS)
                    eng.tensor_tensor(scr, ps[:, 2:4, :].rearrange("p b n -> p (b n)"), G1[:, v, :], ALU.mult
                                      ).then_inc(proj_done, 1)
                    eng.wait_ge(proj_done, t + 1)
                    ins = eng.scalar_tensor_tensor(out=x1[:, t, :], in0=x1[:, t, :], scalar=ALPHA, in1=scr,
                                                   op0=ALU.mult, op1=ALU.add)
                    chain(ins)
                    layer_norm(eng, x1[:, t, :], var_ready, std_ready, t)
                    chain(eng.tensor_tensor(x1[:, t, :], x1[:, t, :], lnG, ALU.mult))
                    eng.tensor_tensor(x1[:, t, :], x1[:, t, :], lnB, ALU.add).then_inc(x1_done, 1)
                eng.wait_ge(logit_ready, TT)
                logits = ps[:, 7, 0:TT * E].rearrange("p (t e) -> p t e", t=TT)
                chain(eng.tensor_reduce(amax, logits, AX_X, ALU.max))
                eng.tensor_tensor(aff, logits, amax.unsqueeze(2).broadcast_to([P, TT, E]), ALU.subtract
                                  ).then_inc(logit_sub, 1)
                eng.wait_ge(aff_exp, 1)
                chain(eng.tensor_reduce(asum, aff, AX_X, ALU.add))
                chain(eng.reciprocal(asum, asum))
                eng.tensor_tensor(aff, aff, asum.unsqueeze(2).broadcast_to([P, TT, E]), ALU.mult
                                  ).then_inc(aff_done, 1)
                eng.wait_ge(afft_ready, 1)
                chain(eng.tensor_copy(affT[0:E, 0:LAT], ps[0:E, 0, :]))
                chain(eng.tensor_copy(affT[0:E, LAT:TOK], ps[0:E, 1, 0:P]))
                for t0, t1, cap in ((0, CTX, CAP_C), (CTX, TOK, CAP_L)):
                    w = affT[0:E, t0:t1]
                    for r in range(cap // 8):
                        chain(eng.max(top8[0:E], w))
                        chain(eng.match_replace(w, top8[0:E], w, -1.0))
                chain(eng.memset(zeros[0:E], 0.0))
                chain(eng.tensor_scalar(picked[0:E], affT[0:E], 0.0, None, ALU.is_lt))
                for t0, t1 in ((0, CTX), (CTX, TOK)):
                    chain(eng.tensor_tensor_scan(work[0:E, t0:t1], picked[0:E, t0:t1], zeros[0:E, t0:t1], 0.0,
                                                 ALU.add, ALU.add))
                eng.tensor_tensor(rank[0:E], work[0:E], picked[0:E], ALU.mult).then_inc(rank_done, 1)
                eng.wait_ge(pos_ready, 1)
                chain(eng.tensor_copy(pos, ps[:, 2, 0:TT * E].rearrange("p (t e) -> p t e", t=TT)))
                for t in range(1, TT):
                    eng.tensor_tensor(selL[:, t - 1], pos[:, t, :].unsqueeze(2).broadcast_to([P, E, CAP_L]),
                                      iota1.unsqueeze(1).broadcast_to([P, E, CAP_L]), ALU.is_equal)
                eng.tensor_tensor(selC, pos[:, 0, :].unsqueeze(2).broadcast_to([P, E, CAP_C]),
                                  iota1[:, 0:CAP_C].unsqueeze(1).broadcast_to([P, E, CAP_C]), ALU.is_equal
                                  ).then_inc(sel_done, 1)

        places.pop().close()
        selG = take(TT * CAP).rearrange("p (t s) -> p t s", t=TT)
        GT = take(TOK)
        X = take(2 * KT * CAP).rearrange("p (e k s) -> p e k s", e=2, k=KT)
        hid = take(2 * 256).rearrange("p (b n) -> p b n", b=2)
        sg = take(2 * 256).rearrange("p (b n) -> p b n", b=2)
        Y = X.rearrange("p e k s -> p (e k s)")[:, 0:D]
        wH, wL = (take(SPLITS * CW, F32R).rearrange("p (b n) -> p b n", b=SPLITS) for _ in range(2))
        xH, xL = (take(2 * KT * CAP, F32R).rearrange("p (e k s) -> p e k s", e=2, k=KT) for _ in range(2))
        hH, hL = (take(FT * CAP, F32R).rearrange("p (f s) -> p f s", f=FT) for _ in range(2))

        gather_ready = sem("gather_ready")
        x_done = sem("x_done")
        xh_done = sem("xh_done")
        xsplit_done = sem("xsplit_done")
        selg_done = sem("selg_done")
        gt_ready = sem("gt_ready")
        gt_copied = sem("gt_copied")
        wh_done = sem("wh_done")
        piece_used = sem("piece_used")
        silu_ready = sem("silu_ready")
        h_ready = sem("h_ready")
        ht_ready = sem("ht_ready")
        hh_done = sem("hh_done")
        hsplit_done = sem("hsplit_done")
        y_copied = sem("y_copied")
        acc_zero = sem("acc_zero")
        PIECES = 3 * NC_F
        S10 = 2 * TT
        G_BANKS = (6, 7, 3)

        def split_count(j, m):
            return j * PER_PAIR + (FIRST_EXPERT_CHUNK + m + 1)

        def used_count(j, m):
            return j * PER_PAIR + (m + 1 + SPLIT_PRIMED)

        with nc.Block() as block:
            @block.sync
            def _(eng):
                eng.sem_inc(piece_used, SPLIT_PRIMED)
                first = ADA_CHUNKS + OUT_CHUNKS + RING
                rounds = (FIRST_EXPERT_CHUNK + EXPERT_CHUNKS - first) // RING
                assert first + rounds * RING == FIRST_EXPERT_CHUNK + EXPERT_CHUNKS
                with eng.Fori(0, rounds) as r:
                    for m in range(RING):
                        n = first + m
                        eng.wait_ge(chunk_used, r * RING + (n - RING + 1))
                        eng.dma_start(ring[:, n % RING, :], a["w_exp"][r * RING + (n - FIRST_EXPERT_CHUNK)]
                                      ).then_inc(landed[n % RING], 16)

            @block.tensor
            def _(eng):
                def three(out, xh, xl, wh, wl, start, stop):
                    eng.matmul(out, xh, wh, start=start, stop=False)
                    eng.matmul(out, xh, wl, start=False, stop=False)
                    return eng.matmul(out, xl, wh, start=False, stop=stop)

                with eng.Fori(0, PAIRS) as j:
                    eng.wait_ge(scat_added, j * 2 * S10 + PRIMED)
                    for k in range(KT):
                        bank, c0 = G_BANKS[k // 3], (k % 3) * 2 * CAP
                        for t in range(1, TT):
                            eng.matmul(ps[:, bank, c0:c0 + 2 * CAP_L], x1[:, t, k * P:(k + 1) * P],
                                       selL[:, t - 1, bass.ds(j * 2, 2), :], start=(t == 1), stop=(t == TT - 1))
                        mm = eng.matmul(ps[:, bank, c0 + 2 * CAP_L:c0 + 2 * CAP], x1[:, 0, k * P:(k + 1) * P],
                                        selC[:, bass.ds(j * 2, 2), :], start=True, stop=True)
                    mm.then_inc(gather_ready, 1)
                    eng.wait_ge(x_done, j * 2 * KT + 2 * KT)
                    eng.wait_ge(xsplit_done, j + 1)

                    def turn(e, q):
                        eng.wait_ge(h_ready, j * 2 * NC_F + e * NC_F + q + 1)
                        if (e, q) >= (0, 2):
                            eng.wait_ge(hsplit_done, j * 2 * NC_F + e * NC_F + q - 1)
                        for f in range(FPC):
                            mm = eng.transpose(ps[:, 2 + q % 2, f * P:f * P + CAP], hid[0:CAP, q % 2, f * P:(f + 1) * P],
                                               ident[0:CAP, 0:CAP])
                        mm.then_inc(ht_ready, 1)

                    for e in range(2):
                        eng.wait_ge(selg_done, j * 2 + e + 1)
                        if e == 1:
                            eng.wait_ge(hsplit_done, j * 2 * NC_F + NC_F)
                        for t in range(TT):
                            out = ps[0:CAP, 2, 0:P] if t == 0 else ps[0:CAP, 3, (t - 1) * P:t * P]
                            mm = eng.transpose(out, selG[:, t, :], ident)
                        mm.then_inc(gt_ready, 1)
                        eng.wait_ge(gt_copied, j * 2 + e + 1)
                        for p in range(PIECES):
                            m = e * PIECES + p
                            b = m % SPLITS
                            if p < 2 * NC_F:
                                q, half = p // 2, p % 2
                                if half == 0 and (e, q) >= (0, 2):
                                    eng.wait_ge(h_ready, j * 2 * NC_F + e * NC_F + q - 1)
                                eng.wait_ge(chunk_used, split_count(j, m))
                                for k in range(KT // 2):
                                    kk = half * (KT // 2) + k
                                    mm = three(ps[0:CAP, q % 2, :], xH[:, e, kk, :], xL[:, e, kk, :],
                                               wH[:, b, k * 512:(k + 1) * 512], wL[:, b, k * 512:(k + 1) * 512],
                                               kk == 0, kk == KT - 1)
                            else:
                                c = p - 2 * NC_F
                                eng.wait_ge(hsplit_done, j * 2 * NC_F + e * NC_F + c + 1)
                                if e == 1 and c == 0:
                                    eng.wait_ge(y_copied, j * 2 + 1)
                                eng.wait_ge(chunk_used, split_count(j, m))
                                for f in range(FPC):
                                    for d in range(2):
                                        w0 = f * D + d * 512
                                        mm = three(ps[0:CAP, 4 + d, :], hH[:, c * FPC + f, :], hL[:, c * FPC + f, :],
                                                   wH[:, b, w0:w0 + 512], wL[:, b, w0:w0 + 512],
                                                   c == 0 and f == 0, c == NC_F - 1 and f == FPC - 1)
                            mm.then_inc(piece_used, 1)
                            if p % 2 == 1 and 3 <= p <= 2 * NC_F + 1:
                                turn(e, (p - 3) // 2)
                        eng.wait_ge(y_copied, j * 2 + e + 1)
                        for s in range(S10):
                            if e or s >= 2:
                                eng.wait_ge(scat_added, j * 2 * S10 + e * S10 + s - 1 + PRIMED)
                            eng.matmul(ps[:, 6 + s % 2, :], GT[0:CAP, (s // 2) * P:(s // 2 + 1) * P],
                                       Y[0:CAP, (s % 2) * 512:(s % 2 + 1) * 512], start=True, stop=True
                                       ).then_inc(scat_ready, 1)

            @block.scalar
            def _(eng):
                with eng.Fori(0, PAIRS) as j:
                    eng.wait_ge(x_done, j * 2 * KT + 2 * KT)
                    flat = "p e k s -> p (e k s)"
                    eng.activation(xH.rearrange(flat), X.rearrange(flat), ACT.Copy).then_inc(xh_done, 1)
                    for e in range(2):
                        for p in range(PIECES):
                            m = e * PIECES + p
                            n = FIRST_EXPERT_CHUNK + m
                            eng.wait_ge(landed[n % RING], j * (16 * PER_PAIR // RING) + 16 * (n // RING + 1))
                            eng.wait_ge(piece_used, used_count(j, m - SPLITS))
                            eng.activation(wH[:, m % SPLITS, :], ring[:, n % RING, :], ACT.Copy).then_inc(wh_done, 1)
                            if p == 1:
                                eng.wait_ge(gt_ready, j * 2 + e + 1)
                                eng.activation(GT[0:CAP, 0:P], ps[0:CAP, 2, 0:P], ACT.Copy)
                                eng.activation(GT[0:CAP, P:TOK], ps[0:CAP, 3, :], ACT.Copy).then_inc(gt_copied, 1)
                            if p % 2 == 1 and 3 <= p <= 2 * NC_F + 1:
                                q = (p - 3) // 2
                                qq = e * NC_F + q
                                eng.wait_ge(piece_used, used_count(j, m - 2))
                                if qq >= 2:
                                    eng.wait_ge(h_ready, j * 2 * NC_F + qq - 1)
                                eng.activation(sg[0:CAP, q % 2, :], ps[0:CAP, q % 2, 0:256], ACT.Silu
                                               ).then_inc(silu_ready, 1)
                            if p % 2 == 1 and 5 <= p <= 2 * NC_F + 3:
                                q = (p - 5) // 2
                                eng.wait_ge(ht_ready, j * 2 * NC_F + e * NC_F + q + 1)
                                src = ps[:, 2 + q % 2, 0:256].rearrange("p (f s) -> p f s", f=FPC)
                                eng.activation(hH[:, q * FPC:(q + 1) * FPC, :], src[:, :, 0:CAP], ACT.Copy
                                               ).then_inc(hh_done, 1)
                        eng.wait_ge(piece_used, used_count(j, (e + 1) * PIECES - 1))
                        eng.activation(Y[0:CAP], ps[0:CAP, 4:6, :].rearrange("p b n -> p (b n)"), ACT.Copy
                                       ).then_inc(y_copied, 1)

            @block.vector
            def _(eng):
                eng.memset(facc.rearrange("p t d -> p (t d)"), 0.0).then_inc(acc_zero, 1)
                eng.memset(selG.rearrange("p t s -> p (t s)"), 0.0).then_inc(acc_zero, 1)
                eng.wait_ge(acc_zero, 2)
                with eng.Fori(0, PAIRS) as j:
                    def scatter_matrix(e):
                        if e == 1:
                            eng.wait_ge(gt_ready, j * 2 + 1)
                        ea = j * 2 + e
                        eng.tensor_tensor(selG[:, 0, CAP_L:CAP].unsqueeze(1), selC[:, bass.ds(ea, 1), :],
                                          aff[:, 0, bass.ds(ea, 1)].unsqueeze(2).broadcast_to([P, 1, CAP_C]), ALU.mult)
                        eng.tensor_tensor(selG[:, 1:TT, 0:CAP_L].unsqueeze(2), selL[:, :, bass.ds(ea, 1), :],
                                          aff[:, 1:TT, bass.ds(ea, 1)].unsqueeze(3).broadcast_to([P, 4, 1, CAP_L]),
                                          ALU.mult).then_inc(selg_done, 1)

                    scatter_matrix(0)
                    eng.wait_ge(gather_ready, j + 1)
                    for k in range(KT):
                        bank, c0 = G_BANKS[k // 3], (k % 3) * 2 * CAP
                        for v, b0, n, s0 in ((1, c0, CAP_L, 0), (0, c0 + 2 * CAP_L, CAP_C, CAP_L)):
                            src = ps[:, bank, b0:b0 + 2 * n].rearrange("p (e s) -> p e s", e=2)
                            eng.tensor_scalar(X[:, :, k, s0:s0 + n], src, modT[:, 4, k, v:v + 1],
                                              modT[:, 3, k, v:v + 1], ALU.mult, ALU.add).then_inc(x_done, 1)
                    eng.wait_ge(xh_done, j + 1)
                    eng.tensor_tensor(xL, X, xH.bitcast(F32), ALU.subtract).then_inc(xsplit_done, 1)
                    for e in range(2):
                        for p in range(PIECES):
                            m = e * PIECES + p
                            n = FIRST_EXPERT_CHUNK + m
                            eng.wait_ge(wh_done, j * PER_PAIR + m + 1)
                            eng.tensor_tensor(wL[:, m % SPLITS, :], ring[:, n % RING, :], wH[:, m % SPLITS, :].bitcast(F32),
                                              ALU.subtract).then_inc(chunk_used, 1)
                            if e == 0 and p == 4:
                                scatter_matrix(1)
                            if p % 2 == 1 and 3 <= p <= 2 * NC_F + 1:
                                q = (p - 3) // 2
                                eng.wait_ge(silu_ready, j * 2 * NC_F + e * NC_F + q + 1)
                                if (e, q) >= (0, 2):
                                    eng.wait_ge(ht_ready, j * 2 * NC_F + e * NC_F + q - 1)
                                eng.tensor_tensor(hid[0:CAP, q % 2, :], sg[0:CAP, q % 2, :],
                                                  ps[0:CAP, q % 2, 256:512], ALU.mult).then_inc(h_ready, 1)
                            if p % 2 == 1 and 5 <= p <= 2 * NC_F + 3:
                                q = (p - 5) // 2
                                eng.wait_ge(hh_done, j * 2 * NC_F + e * NC_F + q + 1)
                                src = ps[:, 2 + q % 2, 0:256].rearrange("p (f s) -> p f s", f=FPC)
                                eng.tensor_tensor(hL[:, q * FPC:(q + 1) * FPC, :], src[:, :, 0:CAP],
                                                  hH[:, q * FPC:(q + 1) * FPC, :].bitcast(F32), ALU.subtract
                                                  ).then_inc(hsplit_done, 1)
                        for s in range(S10):
                            eng.wait_ge(scat_ready, j * 2 * S10 + e * S10 + s + 1 + PRIMED)
                            dst = facc[:, s // 2, (s % 2) * 512:(s % 2 + 1) * 512]
                            eng.tensor_tensor(dst, ps[:, 6 + s % 2, :], dst, ALU.add).then_inc(scat_added, 1)

        var2_ready = sem("var2_ready")
        std2_ready = sem("std2_ready")
        y_done = sem("y_done")
        stored = sem("stored")
        g2_landed = sem("g2_landed")
        G2 = selL.rearrange("p t e s -> p (t e s)")[:, 0:2 * D].rearrange("p (v d) -> p v d", v=2)

        with nc.Block() as block:
            @block.sync
            def _(eng):
                eng.dma_start(G2, gate_scratch[1].rearrange("v k p -> v (k p)").partition_broadcast(P)
                              ).then_inc(g2_landed, 16)
                for t in range(TT):
                    eng.wait_ge(y_done, t + 1)
                    eng.dma_start(a["y"][t], x1[:, t, :]).then_inc(stored, 16)
                eng.wait_ge(stored, 16 * TT)

            @block.scalar
            def _(eng):
                for t in range(TT):
                    eng.wait_ge(var2_ready, t + 1)
                    eng.activation(bnag[:, 2:3], bnag[:, 1:2], ACT.Sqrt).then_inc(std2_ready, 1)

            @block.vector
            def _(eng):
                eng.wait_ge(route_landed, 16 * 6)
                eng.wait_ge(g2_landed, 16)
                for t in range(TT):
                    x, f = x1[:, t, :], facc[:, t, :]
                    chain(eng.tensor_tensor(f, f, G2[:, min(t, 1), :], ALU.mult))
                    chain(eng.scalar_tensor_tensor(out=x, in0=x, scalar=ALPHA, in1=f, op0=ALU.mult, op1=ALU.add))
                    layer_norm(eng, x, var2_ready, std2_ready, t)
                    chain(eng.tensor_tensor(x, x, lnG, ALU.mult))
                    eng.tensor_tensor(x, x, lnB, ALU.add).then_inc(y_done, 1)


def constants():
    j = np.arange(P)
    rot = np.zeros((P, P), np.float32)
    for m in range(P):
        if m % 32 < 16:
            rot[m + 16, m] = -1.0
        else:
            rot[m - 16, m] = 1.0
    t = np.arange(LAT)
    half = HD // 2
    inv = (np.float32(10000.0) ** (-np.arange(0, half, 2, dtype=np.float32) / np.float32(half))).astype(np.float32)
    ang_r = (t // GRID).astype(np.float32)[:, None] * inv[None, :]
    ang_c = (t % GRID).astype(np.float32)[:, None] * inv[None, :]
    ang = np.concatenate([ang_r, ang_r, ang_c, ang_c], axis=1).astype(np.float32)
    cos = np.concatenate([np.cos(ang).T, np.cos(ang).T], axis=0)
    sin = np.concatenate([np.sin(ang).T, np.sin(ang).T], axis=0)
    w = np.arange(GRID)
    c0 = np.clip(w - WIN_W // 2, 0, GRID - WIN_W)
    inside = (w[None, :] >= c0[:, None]) & (w[None, :] < c0[:, None] + WIN_W)
    mask = np.where(inside, 0.0, NEG).astype(np.float32)
    x = np.arange(P)
    hot = (x[None, :] == (GRID + WIN_W - 1) - np.arange(DC)[:, None]).astype(np.float32)
    return {
        "ident": np.eye(P, dtype=np.float32),
        "rotM": rot,
        "cosT": np.ascontiguousarray(cos, dtype=np.float32),
        "sinT": np.ascontiguousarray(sin, dtype=np.float32),
        "mask": np.concatenate([mask, mask], axis=0),
        "iota1": np.tile(np.arange(1, CAP_L + 1, dtype=np.float32), (P, 1)),
        "colhot": hot,
    }


def kernel(**inputs):
    import concourse.bacc as bacc
    from concourse.bass_utils import run_bass_kernel_spmd

    x = {k: np.asarray(v) for k, v in inputs.items()}

    def rows_to_chunks(w, cols):
        return w.reshape(KT, P, -1, cols).transpose(2, 1, 0, 3)

    tokens = np.concatenate([x["x_prompt"][0], x["x_sample"][0]], axis=0)
    w_in = x["w_in"][0].reshape(KT, P, 6, GROUPS, P)
    w_in = np.stack([w_in[:, :, [0, 1]], w_in[:, :, [3, 4]], w_in[:, :, [2, 5]]], axis=0)
    w_in = w_in.transpose(4, 0, 2, 1, 3, 5).reshape(GROUPS, 3, P, KT, 256)
    gate_up = np.stack([x["w_gate"][0].reshape(E, 2, KT // 2, P, NC_F, 256),
                        x["w_up"][0].reshape(E, 2, KT // 2, P, NC_F, 256)], axis=0)
    gate_up = gate_up.transpose(1, 5, 2, 4, 3, 0, 6).reshape(E, 2 * NC_F, P, CW)
    down = x["w_down"][0].reshape(E, NC_F, FPC, P, D).transpose(0, 1, 3, 2, 4).reshape(E, NC_F, P, CW)
    w_exp = np.concatenate([gate_up, down], axis=1).reshape(EXPERT_CHUNKS, P, CW)
    k_na = x["cache_na_k"][0, 0].reshape(GROUPS, 2, CTX, HD).transpose(0, 1, 3, 2).reshape(GROUPS, P, CTX)
    k_df = x["cache_diff_k"][0, 0].transpose(0, 1, 3, 2).reshape(GROUPS, P, CTX)
    v_na = x["cache_na_v"][0, 0].reshape(GROUPS, 2, CTX, HD).transpose(0, 2, 1, 3).reshape(GROUPS, CTX, P)
    v_df = x["cache_diff_v"][0, 0]
    arrays = constants()
    arrays.update({
        "x": tokens.reshape(TT, P, D),
        "xT": tokens.reshape(TOK, KT, P).transpose(2, 1, 0),
        "cvecs": np.stack([x["c_ctx"], x["c"][0]], axis=0).reshape(2, KT, P).transpose(2, 1, 0),
        "b_ada": x["b_ada"][0].reshape(6, KT, P).transpose(2, 0, 1),
        "w_ada": rows_to_chunks(x["w_ada"][0], 256).reshape(ADA_CHUNKS, P, CW),
        "w_out": rows_to_chunks(x["w_out"][0], 256).reshape(OUT_CHUNKS, P, CW),
        "w_in": w_in,
        "w_exp": w_exp,
        "w_router": x["w_router"][0].reshape(KT, P, E).transpose(1, 0, 2),
        "rpbT": x["na_rel_bias"][0].transpose(2, 0, 1),
        "lambdas": np.stack([x["lambda_q1"][0], x["lambda_k1"][0], x["lambda_q2"][0], x["lambda_k2"][0]], axis=0),
        "subln_g": x["subln_g"][0],
        "ln1_g": x["ln1_g"][0], "ln1_b": x["ln1_b"][0], "ln2_g": x["ln2_g"][0], "ln2_b": x["ln2_b"][0],
        "cacheKT": np.stack([k_na, k_df], axis=1),
        "cacheV": np.concatenate([v_na, v_df], axis=2),
    })
    nc = bacc.Bacc("TRN2", target_bir_lowering=False, num_devices=1)
    feed, aps = {}, {}
    for name, value in arrays.items():
        value = np.ascontiguousarray(value)
        feed[f"in_{name}"] = value
        aps[name] = nc.dram_tensor(f"in_{name}", value.shape, mybir.dt.from_np(value.dtype), kind="ExternalInput").ap()
    for name, shape in (("y", (TT, P, D)), ("k_new", (GROUPS, CTX, 256)), ("v_new", (GROUPS, CTX, 256))):
        aps[name] = nc.dram_tensor(f"out_{name}", shape, F32, kind="ExternalOutput").ap()
    build(nc, aps)
    r = run_bass_kernel_spmd(nc, [feed], core_ids=[0]).results[0]
    y, k_new, v_new = r["out_y"], r["out_k_new"], r["out_v_new"]
    y_prompt = y[0].reshape(1, CTX, D)
    y_sample = y[1:].reshape(1, LAT, D)
    na_k = k_new[:, :, :P].reshape(GROUPS, CTX, 2, HD).transpose(0, 2, 1, 3).reshape(1, 1, 2 * GROUPS, CTX, HD)
    na_v = v_new[:, :, :P].reshape(GROUPS, CTX, 2, HD).transpose(0, 2, 1, 3).reshape(1, 1, 2 * GROUPS, CTX, HD)
    df_k = k_new[:, :, P:].reshape(GROUPS, CTX, 2, HD).transpose(0, 2, 1, 3).reshape(1, 1, GROUPS, 2, CTX, HD)
    df_v = v_new[:, :, P:].reshape(1, 1, GROUPS, CTX, P)
    return (y_prompt, y_sample, na_k, na_v, df_k, df_v)
```
